# Optimizing a Trainium2 kernel written in Bass

```python
import math
import jax
import jax.numpy as jnp
from jax import lax
import numpy as np
import jax, jax.numpy as jnp

D_MODEL = 1024
BATCH = 1
SEQ = 512
DEPTH = 1

GRID_W = 64
CTX_LEN = 256
N_GROUPS = 4
GROUP_W = D_MODEL // N_GROUPS
GROUP_HEADS = 4
HEAD_DIM = GROUP_W // GROUP_HEADS
NA_WIN_H = 8
NA_WIN_W = 16
DN_CONV_K = 5
DN_CHUNK = 64
DIFF_DIM = HEAD_DIM // 2
Q_BLOCK = 128
FT_DIM = GROUP_W // GROUP_HEADS
N_EXPERTS = 16
EC_FACTOR = 2
D_EXPERT = 2 * D_MODEL
ROPE_BASE = 10000.0
RMS_EPS = 1e-6
IN_WIDTHS = (GROUP_W, GROUP_W, GROUP_W, 3 * GROUP_W, 2 * GROUP_HEADS, 2 * GROUP_HEADS, GROUP_W, GROUP_W, GROUP_W, GROUP_W, GROUP_W)
IN_W = 11 * GROUP_W + 4 * GROUP_HEADS
F32 = jnp.float32


def rmsnorm(x, g):
    xf = x.astype(F32)
    y = xf * lax.rsqrt(jnp.mean(xf * xf, axis=-1, keepdims=True) + RMS_EPS)
    return (y * g.astype(F32)).astype(x.dtype)

def l2norm(x):
    return x * lax.rsqrt(jnp.sum(x * x, axis=-1, keepdims=True) + 1e-6)

def modulate(h, shift, scale):
    return h * (1 + scale) + shift

def split_heads(t, d=HEAD_DIM):
    return t.reshape(*t.shape[:-1], t.shape[-1] // d, d)

def split_proj(p):
    idx, acc = [], 0
    for w in IN_WIDTHS[:-1]:
        acc += w
        idx.append(acc)
    return jnp.split(p, idx, axis=-1)

def axial_rope(n_tok, dim):
    t = jnp.arange(n_tok)
    pos = jnp.stack([t // GRID_W, t % GRID_W], axis=-1).astype(F32)
    n_freq = dim // 4
    inv = ROPE_BASE ** (-jnp.arange(n_freq, dtype=F32) / n_freq)
    ang = (pos[:, :, None] * inv).reshape(n_tok, 2 * n_freq)
    return jnp.cos(ang), jnp.sin(ang)

def apply_rope(x, cos, sin):
    xf = x.astype(F32).reshape(*x.shape[:-1], -1, 2)
    x1, x2 = xf[..., 0], xf[..., 1]
    out = jnp.stack([x1 * cos - x2 * sin, x1 * sin + x2 * cos], axis=-1)
    return out.reshape(x.shape).astype(x.dtype)

def softmax_attention(q, k, v):
    s = jnp.einsum('bqhd,bkhd->bhqk', q, k).astype(F32) * q.shape[-1] ** -0.5
    p = jax.nn.softmax(s, axis=-1)
    return jnp.einsum('bhqk,bkhd->bqhd', p, v.astype(F32))

def neighbourhood_attention(q, k, v, k_ctx, v_ctx, rpb):
    B, S, H, dh = q.shape
    rows = S // GRID_W
    wh = min(NA_WIN_H, rows)
    r = jnp.arange(rows)
    row_idx = jnp.clip(r - wh // 2, 0, rows - wh)[:, None] + jnp.arange(wh)[None, :]
    cq = jnp.arange(GRID_W)
    c0 = jnp.clip(cq - NA_WIN_W // 2, 0, GRID_W - NA_WIN_W)
    in_win = (cq[None, :] >= c0[:, None]) & (cq[None, :] < c0[:, None] + NA_WIN_W)
    dy = row_idx - r[:, None] + NA_WIN_H - 1
    dx = jnp.clip(cq[None, :] - cq[:, None], 1 - NA_WIN_W, NA_WIN_W - 1) + NA_WIN_W - 1
    bias = rpb[:, dy[:, None, :, None], dx[None, :, None, :]].astype(F32)
    qg = q.reshape(B, rows, GRID_W, H, dh)
    k_blk = k.reshape(B, rows, GRID_W, H, dh)[:, row_idx]
    v_blk = v.reshape(B, rows, GRID_W, H, dh)[:, row_idx]
    scale = dh ** -0.5
    s_win = jnp.einsum('brqhd,brwkhd->bhrqwk', qg, k_blk).astype(F32) * scale + bias
    s_win = jnp.where(in_win[:, None, :], s_win, -jnp.inf)
    s_ctx = jnp.einsum('brqhd,blhd->bhrql', qg, k_ctx).astype(F32) * scale
    n_win = wh * GRID_W
    p = jax.nn.softmax(jnp.concatenate([s_win.reshape(B, H, rows, GRID_W, n_win), s_ctx], axis=-1), axis=-1)
    p_win = p[..., :n_win].reshape(B, H, rows, GRID_W, wh, GRID_W)
    p_ctx = p[..., n_win:]
    out = jnp.einsum('bhrqwk,brwkhd->brqhd', p_win, v_blk.astype(F32)) + jnp.einsum('bhrql,blhd->brqhd', p_ctx, v_ctx.astype(F32))
    return out.reshape(B, S, H, dh)

def short_conv(u, w):
    return lax.conv_general_dilated(u, w[:, None, :].astype(u.dtype), window_strides=(1,), padding=[(DN_CONV_K // 2, DN_CONV_K // 2)], dimension_numbers=('NWC', 'WIO', 'NWC'), feature_group_count=u.shape[-1])

def chunk_gated_delta(q, k, v, g, beta, s0):
    B, T, H, dk = q.shape
    n, C = T // DN_CHUNK, DN_CHUNK

    def chunks(t):
        return jnp.swapaxes(t.reshape(B, n, C, H, *t.shape[3:]), 2, 3)
    qc, kc, vc, bc = chunks(q), chunks(k), chunks(v), chunks(beta)
    gc = jnp.cumsum(chunks(g), axis=-1)
    incl = jnp.tril(jnp.ones((C, C), bool))
    strict = jnp.tril(jnp.ones((C, C), bool), -1)
    decay = jnp.exp(jnp.where(incl, gc[..., :, None] - gc[..., None, :], -jnp.inf))
    kb = kc * bc[..., None]
    lower = jnp.where(strict, jnp.einsum('bnhid,bnhjd->bnhij', kb, kc) * decay, 0.0)
    eye = jnp.eye(C, dtype=F32)
    t_inv = lax.linalg.triangular_solve(eye + lower, jnp.broadcast_to(eye, lower.shape), left_side=True, lower=True, unit_diagonal=True)
    u = t_inv @ (vc * bc[..., None])
    w = t_inv @ (kb * jnp.exp(gc)[..., None])
    qk = jnp.where(incl, jnp.einsum('bnhid,bnhjd->bnhij', qc, kc) * decay, 0.0)
    q_dec = qc * jnp.exp(gc)[..., None]
    k_dec = kc * jnp.exp(gc[..., -1:] - gc)[..., None]
    g_last = jnp.exp(gc[..., -1])

    def step(s, xs):
        u_i, w_i, qk_i, qd_i, kd_i, gl_i = xs
        v_new = u_i - jnp.einsum('bhcd,bhde->bhce', w_i, s)
        o_i = jnp.einsum('bhcd,bhde->bhce', qd_i, s) + jnp.einsum('bhcj,bhje->bhce', qk_i, v_new)
        s = s * gl_i[..., None, None] + jnp.einsum('bhcd,bhce->bhde', kd_i, v_new)
        return s, o_i
    xs = tuple(jnp.swapaxes(t, 0, 1) for t in (u, w, qk, q_dec, k_dec, g_last))
    s_fin, o = lax.scan(step, s0, xs)
    o = jnp.swapaxes(jnp.swapaxes(o, 0, 1), 2, 3).reshape(B, T, H, -1)
    return o, s_fin

def gated_deltanet(lat, ctx, conv_w, a_log, dt_bias, norm_g):
    def prep(qkv, a, b):
        B, T, _ = qkv.shape
        qkv = jax.nn.silu(short_conv(qkv, conv_w)).astype(F32)
        q, k, v = [split_heads(t) for t in jnp.split(qkv, 3, axis=-1)]
        q = l2norm(q) * HEAD_DIM ** -0.5
        k = l2norm(k)
        a = a.astype(F32).reshape(B, T, 2, GROUP_HEADS)
        b = b.astype(F32).reshape(B, T, 2, GROUP_HEADS)
        g = -jnp.exp(a_log.astype(F32)) * jax.nn.softplus(a + dt_bias.astype(F32))
        return q, k, v, g, jax.nn.sigmoid(b)
    ql, kl, vl, gl, bl = prep(lat[0], lat[1], lat[2])
    qc, kc, vc, gc, bc = prep(ctx[0], ctx[1], ctx[2])
    s0 = jnp.zeros((ql.shape[0], GROUP_HEADS, HEAD_DIM, HEAD_DIM), F32)
    flip = lambda t: jnp.flip(t, axis=1)
    oc_f, sc_f = chunk_gated_delta(qc, kc, vc, gc[:, :, 0], bc[:, :, 0], s0)
    ol_f, _ = chunk_gated_delta(ql, kl, vl, gl[:, :, 0], bl[:, :, 0], sc_f)
    oc_b, sc_b = chunk_gated_delta(flip(qc), flip(kc), flip(vc), flip(gc[:, :, 1]), flip(bc[:, :, 1]), s0)
    ol_b, _ = chunk_gated_delta(flip(ql), flip(kl), flip(vl), flip(gl[:, :, 1]), flip(bl[:, :, 1]), sc_b)

    def finish(o, gate):
        y = rmsnorm(o, norm_g) * jax.nn.silu(split_heads(gate.astype(F32)))
        return y.reshape(gate.shape).astype(gate.dtype)
    return finish(ol_f + flip(ol_b), lat[3]), finish(oc_f + flip(oc_b), ctx[3])

def diff_core(q, k, v, lam):
    s = jnp.einsum('bqhmd,bkhmd->bhmqk', q, k).astype(F32) * q.shape[-1] ** -0.5
    p = jax.nn.softmax(s, axis=-1)
    a = p[:, :, 0] - lam * p[:, :, 1]
    return jnp.einsum('bhqk,bkhd->bqhd', a, v.astype(F32))

def fourier_mix(u, w):
    B, T, _ = u.shape
    uf = u.astype(F32).reshape(B, T, GROUP_HEADS, FT_DIM)
    y = jnp.fft.fft2(uf, axes=(1, 3), norm='ortho').real.reshape(B, T, GROUP_W)
    return (y @ w.astype(F32)).astype(u.dtype)

def expert_choice_ffn(h, w_router, w_gate, w_up, w_down):
    B, N, D = h.shape
    cap = EC_FACTOR * N // N_EXPERTS
    aff = jax.nn.softmax((h @ w_router).astype(F32), axis=-1)
    gate, idx = lax.top_k(jnp.swapaxes(aff, 1, 2), cap)
    xg = jax.vmap(lambda hb, ib: hb[ib])(h, idx)
    hid = jax.nn.silu(jnp.einsum('becd,edf->becf', xg, w_gate)) * jnp.einsum('becd,edf->becf', xg, w_up)
    y = jnp.einsum('becf,efd->becd', hid, w_down) * gate[..., None].astype(h.dtype)
    return jax.vmap(lambda yb, ib: jnp.zeros((N, D), yb.dtype).at[ib.reshape(-1)].add(yb.reshape(-1, D)))(y, idx)

def token_mixers(h_lat, h_ctx, w_in, rpb, conv_w, a_log, dt_bias, dn_g, df_lam, lam_init, df_g, ft_w, cos, sin, ctx_out):
    B, S, _ = h_lat.shape
    L = h_ctx.shape[1]
    (na_q, na_k, na_v, dn_qkv, dn_a, dn_b, dn_gate, df_q, df_k, df_v, ft_u) = split_proj(h_lat @ w_in)
    (cna_q, cna_k, cna_v, cdn_qkv, cdn_a, cdn_b, cdn_gate, cdf_q, cdf_k, cdf_v, cft_u) = split_proj(h_ctx @ w_in)
    diff_heads = lambda t: t.reshape(*t.shape[:-1], GROUP_HEADS, 2, DIFF_DIM)
    dt = h_lat.dtype
    o_na = neighbourhood_attention(split_heads(na_q), split_heads(na_k), split_heads(na_v), split_heads(cna_k), split_heads(cna_v), rpb)
    o_dn, c_dn = gated_deltanet((dn_qkv, dn_a, dn_b, dn_gate), (cdn_qkv, cdn_a, cdn_b, cdn_gate), conv_w, a_log, dt_bias, dn_g)
    lq1, lk1, lq2, lk2 = df_lam.astype(F32)
    lam = jnp.exp(jnp.sum(lq1 * lk1)) - jnp.exp(jnp.sum(lq2 * lk2)) + lam_init
    q_d = apply_rope(diff_heads(df_q), cos, sin)
    k_d = apply_rope(diff_heads(df_k), cos, sin)
    kc_d, vc_d = diff_heads(cdf_k), split_heads(cdf_v)
    k_all = jnp.concatenate([kc_d, k_d], axis=1)
    v_all = jnp.concatenate([vc_d, split_heads(df_v)], axis=1)
    q_blocks = jnp.swapaxes(q_d.reshape(B, S // Q_BLOCK, Q_BLOCK, GROUP_HEADS, 2, DIFF_DIM), 0, 1)
    o_df = lax.map(lambda qb: diff_core(qb, k_all, v_all, lam), q_blocks)
    o_df = jnp.swapaxes(o_df, 0, 1).reshape(B, S, GROUP_HEADS, HEAD_DIM)
    diff_out = lambda o: rmsnorm(o, df_g) * (1.0 - lam_init)
    o_ft = fourier_mix(ft_u, ft_w)
    mix_lat = jnp.concatenate([o_na.reshape(B, S, GROUP_W).astype(dt), o_dn.astype(dt), diff_out(o_df).reshape(B, S, GROUP_W).astype(dt), o_ft.astype(dt)], axis=-1)
    if not ctx_out:
        return mix_lat, None
    c_na = softmax_attention(split_heads(cna_q), split_heads(cna_k), split_heads(cna_v))
    c_df = diff_out(diff_core(diff_heads(cdf_q), kc_d, vc_d, lam))
    c_ft = fourier_mix(cft_u, ft_w)
    mix_ctx = jnp.concatenate([c_na.reshape(B, L, GROUP_W).astype(dt), c_dn.astype(dt), c_df.reshape(B, L, GROUP_W).astype(dt), c_ft.astype(dt)], axis=-1)
    return mix_lat, mix_ctx

def first_inputs(seed: int = 0) -> dict:
    key = jax.random.key(seed)
    ks = jax.random.split(key, 24)
    nrm = lambda k, shape, s: jax.random.normal(k, shape, F32) * s
    H = GROUP_HEADS
    a_init = jax.random.uniform(ks[9], (DEPTH, 2, H), F32, 1.0, 16.0)
    dt_init = jnp.exp(jax.random.uniform(ks[10], (DEPTH, 2, H), F32, math.log(1e-3), math.log(1e-1)))
    return {
        'x': nrm(ks[0], (BATCH, SEQ, D_MODEL), 1.0),
        'c': nrm(ks[1], (BATCH, D_MODEL), 1.0),
        'ctx': nrm(ks[2], (BATCH, CTX_LEN, D_MODEL), 1.0),
        'c_ctx': nrm(ks[3], (D_MODEL,), 1.0),
        'w_mod': nrm(ks[4], (DEPTH, D_MODEL, 6 * D_MODEL), 0.5 * D_MODEL ** -0.5),
        'b_mod': nrm(ks[5], (DEPTH, 6 * D_MODEL), 0.01),
        'norm1_g': 1.0 + nrm(ks[6], (DEPTH, D_MODEL), 0.02),
        'w_in': nrm(ks[7], (DEPTH, D_MODEL, IN_W), D_MODEL ** -0.5),
        'na_rpb': nrm(ks[8], (DEPTH, H, 2 * NA_WIN_H - 1, 2 * NA_WIN_W - 1), 0.02),
        'dn_conv_w': nrm(ks[11], (DEPTH, DN_CONV_K, 3 * GROUP_W), DN_CONV_K ** -0.5),
        'dn_a_log': jnp.log(a_init),
        'dn_dt_bias': dt_init + jnp.log(-jnp.expm1(-dt_init)),
        'dn_norm_g': 1.0 + nrm(ks[12], (DEPTH, HEAD_DIM), 0.02),
        'df_lambda': nrm(ks[13], (DEPTH, 4, DIFF_DIM), 0.1),
        'df_norm_g': 1.0 + nrm(ks[14], (DEPTH, HEAD_DIM), 0.02),
        'ft_w': nrm(ks[15], (DEPTH, GROUP_W, GROUP_W), GROUP_W ** -0.5),
        'w_out': nrm(ks[16], (DEPTH, D_MODEL, D_MODEL), D_MODEL ** -0.5),
        'norm2_g': 1.0 + nrm(ks[17], (DEPTH, D_MODEL), 0.02),
        'w_router': nrm(ks[18], (DEPTH, D_MODEL, N_EXPERTS), D_MODEL ** -0.5),
        'w_gate': nrm(ks[19], (DEPTH, N_EXPERTS, D_MODEL, D_EXPERT), D_MODEL ** -0.5),
        'w_up': nrm(ks[20], (DEPTH, N_EXPERTS, D_MODEL, D_EXPERT), D_MODEL ** -0.5),
        'w_down': nrm(ks[21], (DEPTH, N_EXPERTS, D_EXPERT, D_MODEL), D_EXPERT ** -0.5),
        'final_norm_g': 1.0 + nrm(ks[22], (D_MODEL,), 0.02),
    }

def first_block(x, c, ctx, c_ctx, w_mod, b_mod, norm1_g, w_in, na_rpb, dn_conv_w, dn_a_log, dn_dt_bias, dn_norm_g, df_lambda, df_norm_g, ft_w, w_out, norm2_g, w_router, w_gate, w_up, w_down, final_norm_g):
    S = x.shape[1]
    cos, sin = axial_rope(S, DIFF_DIM)
    cos, sin = cos[:, None, None, :], sin[:, None, None, :]
    s_lat = jax.nn.silu(c)
    s_ctx = jax.nn.silu(c_ctx)
    x_lat, x_ctx = x, ctx
    for l in range(DEPTH):
        ctx_out = l < DEPTH - 1
        lam_init = 0.8 - 0.6 * math.exp(-0.3 * l)
        m_lat = jnp.split((s_lat @ w_mod[l] + b_mod[l])[:, None, :], 6, axis=-1)
        m_ctx = jnp.split(s_ctx @ w_mod[l] + b_mod[l], 6, axis=-1)
        h_lat = modulate(rmsnorm(x_lat, norm1_g[l]), m_lat[0], m_lat[1])
        h_ctx = modulate(rmsnorm(x_ctx, norm1_g[l]), m_ctx[0], m_ctx[1])
        mix_lat, mix_ctx = token_mixers(h_lat, h_ctx, w_in[l], na_rpb[l], dn_conv_w[l], dn_a_log[l], dn_dt_bias[l], dn_norm_g[l], df_lambda[l], lam_init, df_norm_g[l], ft_w[l], cos, sin, ctx_out)
        x_lat = x_lat + m_lat[2] * (mix_lat @ w_out[l])
        h_lat = modulate(rmsnorm(x_lat, norm2_g[l]), m_lat[3], m_lat[4])
        x_lat = x_lat + m_lat[5] * expert_choice_ffn(h_lat, w_router[l], w_gate[l], w_up[l], w_down[l])
        if ctx_out:
            x_ctx = x_ctx + m_ctx[2] * (mix_ctx @ w_out[l])
            h_ctx = modulate(rmsnorm(x_ctx, norm2_g[l]), m_ctx[3], m_ctx[4])
            x_ctx = x_ctx + m_ctx[5] * expert_choice_ffn(h_ctx, w_router[l], w_gate[l], w_up[l], w_down[l])
    return rmsnorm(x_lat, final_norm_g)


DEPTH_2 = 2

MIX_WIDTH = D_MODEL
MLA_WIDTH = D_MODEL // 2
SGU_WIDTH = D_MODEL // 4
POOL_WIDTH = D_MODEL // 4

MLA_HEADS = 4
V_HEAD = MLA_WIDTH // MLA_HEADS
QK_NOPE = 64
QK_ROPE = 32
QK_HEAD = QK_NOPE + QK_ROPE
Q_LORA = D_MODEL // 4
KV_LORA = D_MODEL // 8
ROPE_THETA = 10000.0

SGU_HEADS = 4
SGU_HEAD_DIM = SGU_WIDTH // SGU_HEADS
CHUNK = 128

POOL_WINDOWS = (2, 4, 8, 16)
POOL_GROUPS = len(POOL_WINDOWS)
POOL_GROUP_DIM = POOL_WIDTH // POOL_GROUPS

IN_WIDTH = Q_LORA + KV_LORA + QK_ROPE + 2 * SGU_WIDTH + POOL_WIDTH
FFN_HIDDEN = -(-8 * D_MODEL // (3 * 256)) * 256
EPS = 1e-6


def rms_norm(x, g):
    xf = x.astype(jnp.float32)
    y = xf * lax.rsqrt(jnp.mean(xf * xf, axis=-1, keepdims=True) + EPS)
    return (y * g.astype(jnp.float32)).astype(x.dtype)

def apply_rope_2(x, positions):
    half = x.shape[-1] // 2
    inv_freq = 1.0 / (ROPE_THETA ** (jnp.arange(half, dtype=jnp.float32) / half))
    ang = positions.astype(jnp.float32)[:, :, None, None] * inv_freq
    cos, sin = jnp.cos(ang), jnp.sin(ang)
    xf = x.astype(jnp.float32)
    x1, x2 = xf[..., :half], xf[..., half:]
    return jnp.concatenate([x1 * cos - x2 * sin, x2 * cos + x1 * sin], axis=-1).astype(x.dtype)

def mla_mixer(q_lat, kv_lat, k_rope, positions, g_q_lat, w_q_up, g_kv_lat, w_kv_up, g_q_head, g_k_head):
    B, S, _ = q_lat.shape
    q = (rms_norm(q_lat, g_q_lat) @ w_q_up).reshape(B, S, MLA_HEADS, QK_HEAD)
    kv = (rms_norm(kv_lat, g_kv_lat) @ w_kv_up).reshape(B, S, MLA_HEADS, QK_NOPE + V_HEAD)
    k_nope, v = kv[..., :QK_NOPE], kv[..., QK_NOPE:]
    k_pe = jnp.broadcast_to(k_rope[:, :, None, :], (B, S, MLA_HEADS, QK_ROPE))
    k = jnp.concatenate([k_nope, k_pe], axis=-1)
    q = rms_norm(q, g_q_head)
    k = rms_norm(k, g_k_head)
    q = jnp.concatenate([q[..., :QK_NOPE], apply_rope_2(q[..., QK_NOPE:], positions)], axis=-1)
    k = jnp.concatenate([k[..., :QK_NOPE], apply_rope_2(k[..., QK_NOPE:], positions)], axis=-1)

    n_blocks = S // Q_BLOCK
    scale = 1.0 / math.sqrt(QK_HEAD)
    qb = q.reshape(B, n_blocks, Q_BLOCK, MLA_HEADS, QK_HEAD).transpose(1, 0, 2, 3, 4)
    kpos = jnp.arange(S)

    def attend_block(args):
        qi, bi = args
        s = jnp.einsum('bqhd,bkhd->bhqk', qi, k).astype(jnp.float32) * scale
        qpos = bi * Q_BLOCK + jnp.arange(Q_BLOCK)
        causal = kpos[None, :] <= qpos[:, None]
        s = jnp.where(causal[None, None], s, jnp.finfo(jnp.float32).min)
        p = jax.nn.softmax(s, axis=-1)
        return jnp.einsum('bhqk,bkhd->bqhd', p.astype(v.dtype), v)

    o = lax.map(attend_block, (qb, jnp.arange(n_blocks)))
    return o.transpose(1, 0, 2, 3, 4).reshape(B, S, MLA_WIDTH)

def sgu_mixer(uv, g_v, w_spatial, b_spatial):
    B, S, _ = uv.shape
    u, v = uv[..., :SGU_WIDTH], uv[..., SGU_WIDTH:]
    v = rms_norm(v, g_v)
    vc = v.reshape(B, S // CHUNK, CHUNK, SGU_HEADS, SGU_HEAD_DIM)
    w = w_spatial * jnp.tril(jnp.ones((CHUNK, CHUNK), dtype=w_spatial.dtype))
    zc = jnp.einsum('hts,bcshd->bcthd', w, vc) + b_spatial.T[None, None, :, :, None]
    return u * zc.reshape(B, S, SGU_WIDTH)

def pool_mixer(p, w_pool, pool_scale):
    B, S, _ = p.shape
    pf = p.astype(jnp.float32).reshape(B, S, POOL_GROUPS, POOL_GROUP_DIM)
    t1 = jnp.arange(1, S + 1, dtype=jnp.float32)
    outs = []
    for g, win in enumerate(POOL_WINDOWS):
        xg = pf[:, :, g]
        cs = jnp.cumsum(xg, axis=1)
        cs_shift = jnp.pad(cs, ((0, 0), (win, 0), (0, 0)))[:, :S]
        count = jnp.minimum(t1, float(win))[None, :, None]
        outs.append((cs - cs_shift) / count - xg)
    m = jnp.stack(outs, axis=2).astype(p.dtype)
    y = jnp.einsum('bsgc,gcd->bsgd', m, w_pool).reshape(B, S, POOL_WIDTH)
    return y * pool_scale

def second_inputs(seed: int = 0) -> dict:
    key = jax.random.key(seed)
    ks = jax.random.split(key, 24)
    f32 = jnp.float32

    def dense(k, shape, fan_in):
        return jax.random.normal(k, shape, f32) * fan_in ** -0.5

    def gain(k, shape):
        return 1.0 + 0.01 * jax.random.normal(k, shape, f32)

    x = jax.random.normal(ks[0], (BATCH, SEQ, D_MODEL), f32)
    start = jax.random.randint(ks[1], (BATCH, 1), 0, 4096, dtype=jnp.int32)
    positions = start + jnp.arange(SEQ, dtype=jnp.int32)[None, :]
    return {
        "x": x,
        "positions": positions,
        "g_mix_norm": gain(ks[2], (DEPTH_2, D_MODEL)),
        "w_in": dense(ks[3], (DEPTH_2, D_MODEL, IN_WIDTH), D_MODEL),
        "g_q_lat": gain(ks[4], (DEPTH_2, Q_LORA)),
        "w_q_up": dense(ks[5], (DEPTH_2, Q_LORA, MLA_HEADS * QK_HEAD), Q_LORA),
        "g_kv_lat": gain(ks[6], (DEPTH_2, KV_LORA)),
        "w_kv_up": dense(ks[7], (DEPTH_2, KV_LORA, MLA_HEADS * (QK_NOPE + V_HEAD)), KV_LORA),
        "g_q_head": gain(ks[8], (DEPTH_2, QK_HEAD)),
        "g_k_head": gain(ks[9], (DEPTH_2, QK_HEAD)),
        "g_sgu_v": gain(ks[10], (DEPTH_2, SGU_WIDTH)),
        "w_spatial": dense(ks[11], (DEPTH_2, SGU_HEADS, CHUNK, CHUNK), CHUNK),
        "b_spatial": 1.0 + 0.01 * jax.random.normal(ks[12], (DEPTH_2, SGU_HEADS, CHUNK), f32),
        "w_pool": dense(ks[13], (DEPTH_2, POOL_GROUPS, POOL_GROUP_DIM, POOL_GROUP_DIM), POOL_GROUP_DIM),
        "pool_scale": 1.0 + 0.1 * jax.random.normal(ks[14], (DEPTH_2, POOL_WIDTH), f32),
        "g_out_mla": gain(ks[15], (DEPTH_2, MLA_WIDTH)),
        "g_out_sgu": gain(ks[16], (DEPTH_2, SGU_WIDTH)),
        "g_out_pool": gain(ks[17], (DEPTH_2, POOL_WIDTH)),
        "w_out": dense(ks[18], (DEPTH_2, MIX_WIDTH, D_MODEL), MIX_WIDTH),
        "g_ffn_norm": gain(ks[19], (DEPTH_2, D_MODEL)),
        "w_gate": dense(ks[20], (DEPTH_2, D_MODEL, FFN_HIDDEN), D_MODEL),
        "w_up": dense(ks[21], (DEPTH_2, D_MODEL, FFN_HIDDEN), D_MODEL),
        "w_down": dense(ks[22], (DEPTH_2, FFN_HIDDEN, D_MODEL), FFN_HIDDEN),
    }

def second_block(x, positions, g_mix_norm, w_in, g_q_lat, w_q_up, g_kv_lat, w_kv_up, g_q_head, g_k_head,
              g_sgu_v, w_spatial, b_spatial, w_pool, pool_scale, g_out_mla, g_out_sgu, g_out_pool,
              w_out, g_ffn_norm, w_gate, w_up, w_down):
    o1 = Q_LORA
    o2 = o1 + KV_LORA
    o3 = o2 + QK_ROPE
    o4 = o3 + 2 * SGU_WIDTH
    for l in range(DEPTH_2):
        h = rms_norm(x, g_mix_norm[l])
        z = h @ w_in[l]
        q_lat, kv_lat, k_rope = z[..., :o1], z[..., o1:o2], z[..., o2:o3]
        uv, pin = z[..., o3:o4], z[..., o4:]
        a = mla_mixer(q_lat, kv_lat, k_rope, positions, g_q_lat[l], w_q_up[l], g_kv_lat[l],
                      w_kv_up[l], g_q_head[l], g_k_head[l])
        gm = sgu_mixer(uv, g_sgu_v[l], w_spatial[l], b_spatial[l])
        po = pool_mixer(pin, w_pool[l], pool_scale[l])
        mix = jnp.concatenate([rms_norm(a, g_out_mla[l]), rms_norm(gm, g_out_sgu[l]),
                               rms_norm(po, g_out_pool[l])], axis=-1)
        x = x + mix @ w_out[l]
        h = rms_norm(x, g_ffn_norm[l])
        x = x + (jax.nn.silu(h @ w_gate[l]) * (h @ w_up[l])) @ w_down[l]
    return x


def setup_inputs(seed=0):
    out = dict(first_inputs(seed))
    for name, value in second_inputs(seed + 1).items():
        if name != "x":
            out[name + "_2"] = value
    return out


def reference(
    x, c, ctx, c_ctx, w_mod, b_mod, norm1_g, w_in, na_rpb, dn_conv_w, dn_a_log, dn_dt_bias,
    dn_norm_g, df_lambda, df_norm_g, ft_w, w_out, norm2_g, w_router, w_gate, w_up, w_down,
    final_norm_g, positions_2, g_mix_norm_2, w_in_2, g_q_lat_2, w_q_up_2, g_kv_lat_2, w_kv_up_2,
    g_q_head_2, g_k_head_2, g_sgu_v_2, w_spatial_2, b_spatial_2, w_pool_2, pool_scale_2,
    g_out_mla_2, g_out_sgu_2, g_out_pool_2, w_out_2, g_ffn_norm_2, w_gate_2, w_up_2, w_down_2,
):
    x = first_block(
        x, c, ctx, c_ctx, w_mod, b_mod, norm1_g, w_in, na_rpb, dn_conv_w, dn_a_log, dn_dt_bias,
        dn_norm_g, df_lambda, df_norm_g, ft_w, w_out, norm2_g, w_router, w_gate, w_up, w_down,
        final_norm_g,
    )
    return second_block(
        x, positions_2, g_mix_norm_2, w_in_2, g_q_lat_2, w_q_up_2, g_kv_lat_2, w_kv_up_2,
        g_q_head_2, g_k_head_2, g_sgu_v_2, w_spatial_2, b_spatial_2, w_pool_2, pool_scale_2,
        g_out_mla_2, g_out_sgu_2, g_out_pool_2, w_out_2, g_ffn_norm_2, w_gate_2, w_up_2,
        w_down_2,
    )


_drawn_inputs = setup_inputs


def setup_inputs(seed=0):
    import zlib

    import numpy as np

    out = dict(_drawn_inputs(seed))
    spreads = {}
    factors = {'norm1_g': 7.694,
     'na_rpb': 8.0,
     'dn_norm_g': 8.0,
     'df_lambda': 2.713,
     'df_norm_g': 6.4,
     'norm2_g': 7.406,
     'g_mix_norm_2': 4.873,
     'g_q_lat_2': 8.0,
     'g_kv_lat_2': 6.162,
     'g_q_head_2': 8.0,
     'g_k_head_2': 8.0,
     'g_sgu_v_2': 48.674,
     'b_spatial_2': 37.865,
     'g_out_mla_2': 22.895,
     'g_out_sgu_2': 29.886,
     'g_out_pool_2': 28.842,
     'g_ffn_norm_2': 7.611}
    for name, (base, spread) in spreads.items():
        noise = np.random.default_rng([zlib.crc32(name.encode()), seed]).standard_normal(out[name].shape)
        drawn = base * np.exp(spread * noise) if base else spread * noise
        out[name] = jnp.asarray(drawn.astype(out[name].dtype))
    for name, factor in factors.items():
        out[name] = (out[name] * factor).astype(out[name].dtype)
    return out
```

```python
from contextlib import ExitStack

import numpy as np

import concourse.bass as bass
from concourse import mybir

F32 = mybir.dt.float32
I32 = mybir.dt.int32
ALU = mybir.AluOpType
ACT = mybir.ActivationFunctionType
LN_EXP, SILU = "natural_log_exp_and_others", "silu_and_others"
AX_X = mybir.AxisListType.X

P = 128
D = 1024
KD = D // P
T = 512
L = 256
TT = T // P
ALLT = T + L
H = 4
HD = 64
GW = H * HD
GRID = 64
NDX = 31
CONV = 5
PAD = CONV // 2
CH = 64
NE, CAP = 16, 64
EPS = 1e-6
NEG = -1e30
LAM_INIT = 0.8 - 0.6 * 1.0
SLOT = 4096
SLOTS = 4

L_PAR, L_WQ, L_WKV, L_WPOOL, L_WSP, L_BSP, L_ALL = 40, 40, 808, 1576, 1704, 2216, 2472
TWO_PI = (6.28125, 0.00193500518798828125, 3.0199159819e-07)
LAYERS = 2
QK_NOPE, QK_ROPE, VH = 64, 32, 128
QK_HEAD = QK_NOPE + QK_ROPE
ROPE_THETA = 10000.0
POOL_WIN = np.array([2, 4, 8, 16])
FF = 2816
FT = FF // P

C_COND, C_BMOD, C_N1, C_N2, C_NF, C_CONV, C_DNG, C_DFG, C_SEL = 0, 16, 64, 72, 80, 88, 118, 119, 120
C_ALL = 122
R_ALOG, R_DT, R_LAM, R_ALL = 0, 8, 16, 144


def first_constants():
    f = np.float32
    p = np.arange(P)
    parts = {}
    tok = np.arange(T)
    pos = np.stack([tok // GRID, tok % GRID], -1).astype(f)
    nf = 8
    inv = (f(10000.0) ** (-np.arange(nf, dtype=f) / f(nf))).astype(f)
    ang = (pos[:, :, None] * inv).reshape(T, 16).astype(f)
    pair = (p % 32) // 2
    parts["rope_cos"] = np.cos(ang)[:, pair].T
    parts["rope_sin"] = np.sin(ang)[:, pair].T
    rot = np.zeros((P, P))
    rot[p[1::2], p[0::2]] = -1.0
    rot[p[0::2], p[1::2]] = 1.0
    parts["rope_turn"] = rot
    c = np.arange(HD)
    w = 2 * np.pi * np.outer(c, c) / HD
    s = 1.0 / np.sqrt(T * HD)
    chan = np.zeros((P, 2, P))
    for b in range(2):
        r = slice(b * HD, b * HD + HD)
        chan[r, 0, r] = np.cos(w) * s
        chan[r, 1, r] = np.sin(w) * s
    parts["dft_chan"] = chan.reshape(P, 2 * P)
    cq, ck = p % GRID, np.arange(GRID)
    c0 = np.clip(cq - 8, 0, GRID - 16)
    seen = (ck[None] >= c0[:, None]) & (ck[None] < c0[:, None] + 16)
    parts["na_mask"] = np.where(seen, 0.0, NEG)
    same = (p[:, None] // CH) == (p[None] // CH)
    parts["tri"] = np.concatenate([same & (p[:, None] <= p[None]), same & (p[:, None] >= p[None])], 1)
    i = p % CH
    j = np.arange(CH)
    parts["tri64"] = np.concatenate([i[:, None] <= j[None], i[:, None] >= j[None]], 1)
    parts["same"] = same
    levels = np.zeros((P, 6, 2, CH))
    for lv in range(6):
        b = 1 << lv
        blk = (i[:, None] // (2 * b)) == (j[None] // (2 * b))
        lo_i, lo_j = (i[:, None] // b) % 2 == 0, (j[None] // b) % 2 == 0
        levels[:, lv, 0] = blk & lo_i & ~lo_j
        levels[:, lv, 1] = blk & ~lo_i & lo_j
    parts["levels"] = levels.reshape(P, -1)
    parts["incl"] = np.concatenate([np.where(i[:, None] <= j[None], 0, NEG), np.where(i[:, None] >= j[None], 0, NEG)], 1)
    parts["eye64"] = i[:, None] == j[None]
    at, cols = 0, {}
    for k, v in parts.items():
        cols[k] = (at, at + v.shape[1])
        at += v.shape[1]
    return np.concatenate([v.astype(f) for v in parts.values()], 1), cols


def later_constants():
    f = np.float32
    p = np.arange(P)
    parts = {"iota": np.broadcast_to(np.arange(CAP), (P, CAP))}
    t1 = np.arange(1, T + 1)
    parts["pool_recip"] = np.stack([1.0 / np.minimum(t1[None], POOL_WIN[2 * i + p // HD][:, None]) for i in range(2)], 1).reshape(P, -1)
    turn = np.zeros((P, P))
    j = np.arange(QK_ROPE // 2)
    turn[QK_NOPE + 16 + j, QK_NOPE + j] = -1.0
    turn[QK_NOPE + j, QK_NOPE + 16 + j] = 1.0
    parts["turn"] = turn
    parts["causal"] = np.where(p[None] <= p[:, None], 0.0, NEG)
    parts["keep"] = p[:, None] <= p[None]
    inv = f(1.0) / (f(ROPE_THETA) ** (np.arange(16, dtype=f) / f(16)))
    rope = (p >= QK_NOPE) & (p < QK_HEAD)
    parts["inv_freq"] = np.where(rope, inv[(p - QK_NOPE) % 16], 0.0)[:, None]
    at, cols = 0, {}
    for k, v in parts.items():
        cols[k] = (at, at + v.shape[1])
        at += v.shape[1]
    return np.concatenate([np.asarray(v, dtype=f) for v in parts.values()], 1), cols


def dft_table():
    t = np.arange(T)
    w = 2 * np.pi * (np.outer(t, t) % T) / T
    return np.stack([np.cos(w), -np.sin(w)]).astype(np.float32)


def spread(ap, axis, n):
    shape = list(ap.shape)
    shape.insert(axis, n)
    return ap.unsqueeze(axis).broadcast_to(shape)


class Turn:

    def __init__(self, eng, turn, per, before=None):
        self.eng, self.turn, self.per, self.before, self.at, self.made = eng, turn, per, before or {}, {}, {}

    def upto(self, s, k):
        assert 1 <= k <= self.per[s.name], (s.name, k)
        self.eng.wait_ge(s, self.turn * self.per[s.name] + (self.before.get(s.name, 0) + k))

    def wait(self, s, n=1):
        self.at[s.name] = self.at.get(s.name, 0) + n
        self.upto(s, self.at[s.name])

    def sig(self, ins, s):
        ins.then_inc(s, 1)
        self.made[s.name] = self.made.get(s.name, 0) + 1

    def mark(self, ins, s):
        self.sig(ins, s)
        self.upto(s, self.made[s.name])

    def end(self):
        for k, n in self.made.items():
            assert self.per[k] == n, (k, n, self.per[k])


class Steps:

    def __init__(self, eng):
        self.eng, self.at, self.reg, self.per, self.start = eng, {}, None, {}, {}

    def value(self, s, back=0):
        v = self.at.get(s.name, 0) - back
        if self.reg is not None and self.per.get(s.name):
            return self.reg * self.per[s.name] + v
        return v

    def wait(self, s, n=1):
        self.at[s.name] = self.at.get(s.name, 0) + n
        self.eng.wait_ge(s, self.value(s))

    def mark(self, ins, s):
        ins.then_inc(s, 1)
        self.wait(s)

    def note(self, ins, s):
        ins.then_inc(s, 1)
        self.at[s.name] = self.at.get(s.name, 0) + 1


def build(nc, a, out):
    ctx = ExitStack()
    _, cc = first_constants()

    def sb(name, shape, dt=F32):
        return ctx.enter_context(nc.sbuf_tensor(name, shape, dt))

    def sem(name):
        return ctx.enter_context(nc.semaphore(name))

    xT = sb("xT", [P, KD, T])
    ring = sb("ring", [P, SLOTS, SLOT])
    work = sb("work", [P, 31200])
    ident = sb("ident", [P, P])
    ones = sb("ones", [P, P])
    eps = sb("eps", [P, 2])
    par = sb("par", [P, C_ALL])
    rows = sb("rows", [P, R_ALL])
    mod = sb("mod", [P, 2, KD, 2])
    mod2 = sb("mod2", [P, 4, KD])
    gscale = sb("gscale", [P, KD, 2])
    decay_in = sb("decay_in", [P, 96])
    stat = sb("stat", [P, 64])
    ftw = sb("ftw", [P, 2, GW])
    ps = [ctx.enter_context(nc.psum_tensor(f"pair{i}", [P, 2, 512], F32)) for i in range(4)]
    bank = [ps[i // 2][:, i % 2, :] for i in range(8)]

    def region(at, *dims):
        n = int(np.prod(dims))
        v = work[:, at:at + n]
        if len(dims) == 1:
            return v
        names = "abcd"[:len(dims)]
        return v.rearrange(f"p ({' '.join(names)}) -> p {' '.join(names)}", **dict(zip(names, dims)))

    hL, hC = region(0, KD, T), region(4096, KD, L)
    q_na, k_na, v_na = region(6144, 2, T), region(7168, 2, ALLT), region(8704, 6, GW)
    q_df, k_df, v_df = region(10240, 2, T), region(11264, 2, ALLT), region(12800, 6, GW)
    gate, uft = region(14336, 2, T), region(15360, 2, T)
    dq, dk, dv = region(16384, 2, T), region(17408, 2, ALLT), region(18944, 2, ALLT)
    mix = region(20480, KD, T)
    const = region(24576, 2944)
    rpb = region(27520, H, 14, GRID)
    sqL, sqC = region(6144, KD, T), region(10240, KD, L)
    condw, mod_row = region(23576, KD, 32), region(23832, 512)
    cond_sel = par[:, C_SEL:C_SEL + 2]
    cinL = [region(20480 + i * 516, 516) for i in range(6)]
    cinC = [region(27520 + i * 260, 260) for i in range(4)]
    tab = {k: const[:, lo:hi] for k, (lo, hi) in cc.items()}
    ab = decay_in[:].rearrange("p (t c) -> p t c", t=6)

    PER_E_NAMES = ["pick_ready", "gathered", "pgT_done", "x_tok_ready", "xgT_done", "xg_ready", "pgT_ready", "w_used",
                   "silu_ready", "hid_ready", "hidT_done", "hidT_ready", "y_ready", "scattered", "added", "moe_step"]
    PER_L = dict(l_in=16, l_sq=35, l_sum=15, l_rstd=15, l_h=16, lin_done=24, lin_taken=24, v_rstd=1, v_scaled=4,
                 wsp_ready=1, sgu_done=2, qn_ready=3, kpe_ready=4, pool_ready=1, pool_done=2, pool_taken=2,
                 turn_in=8, turned=8, by_cos=8, roped=8, sc_done=16, sc_taken=16, mx_ready=16, ex_ready=16, pr_ready=16,
                 tr_done=16, pt_taken=16, pvl_done=4, pvl_taken=4, mixn=8, lo_done=8, lo_taken=8,
                 gate_done=22, up_done=22, silu_l=22, hidden=22, down_done=8, down_taken=8,
                 l_act=20, l_dve=56, l_pool=11, pad_ready=1)
    s_par, s_x, s_const, s_bias, s_ftw = (sem(n) for n in ("par_in", "x_in", "const_in", "bias_in", "ftw_in"))
    slot_in = [sem(f"slot{i}_in") for i in range(SLOTS)]
    init_done = sem("init_done")
    cond_ready = sem("cond_ready")
    squares = sem("squares_ready")
    summed = sem("squares_summed")
    rstd_ready = sem("rstd_ready")
    normed = sem("normed")
    mod_done, mod_copied, mod_turned = sem("mod_summed"), sem("mod_copied"), sem("mod_turned")
    mod_taken = sem("mod_taken")
    scaled = sem("scaled_ready")
    h_ready = sem("h_ready")
    proj_done = sem("proj_done")
    proj_taken = sem("proj_taken")
    conv_done = sem("conv_done")
    silu_done = sem("silu_done")
    dve_step, act_step = sem("dve_step"), sem("act_step")
    lam_ready = sem("lam_ready")
    score_ready = sem("scores_ready")
    na_scores_taken, na_max_ready, na_exp_ready = sem("na_scores_taken"), sem("na_max_ready"), sem("na_exp_ready")
    df_max_ready, df_exp_ready = sem("df_max_ready"), sem("df_exp_ready")
    probs_ready = sem("probs_ready")
    transposed = sem("probs_transposed")
    probsT_act, probsT_dve = sem("probsT_taken_act"), sem("probsT_taken_dve")
    pv_done, pv_taken = sem("pv_done"), sem("pv_taken")
    dfo_scaled = sem("dfo_scaled")
    ft_chan_done, ft_chan_taken = sem("ft_chan_done"), sem("ft_chan_taken")
    ft_tok_done, ft_tok_taken = sem("ft_tok_done"), sem("ft_tok_taken")
    ft_done, ft_taken = sem("ft_done"), sem("ft_taken")
    ab_exp, ab_ready = sem("ab_exp"), sem("ab_ready")
    g_ready, gc_done, gc_ready, gc_exp, dn_coef = sem("g_ready"), sem("gc_done"), sem("gc_ready"), sem("gc_exp"), sem("dn_coef")
    tok_done, tok_taken = sem("dn_tok_done"), sem("dn_tok_taken")
    gtri_ready, grow_done, decay_arg, decay_ready = sem("gtri_ready"), sem("grow_done"), sem("decay_arg"), sem("decay_ready")
    kk_done, nt_ready, qk_ready = sem("kk_done"), sem("nt_ready"), sem("qk_ready")
    gb_ready, gq_done, gq_exp = sem("gb_ready"), sem("gq_done"), sem("gq_exp")
    ns_ready = sem("ns_ready")
    y_done, y_ready, x_done, x_ready, w_done, w_ready = (sem(n) for n in
        ("y_done", "yn_ready", "x_done", "x_ready", "w_done", "w_ready"))
    out_done, out_taken = sem("out_done"), sem("out_taken")
    s_later, s_wr = sem("later_in"), sem("w_router_in")
    h2_ready = sem("h2_ready")
    tok2_done, tok2_taken = sem("tok2_done"), sem("tok2_taken")
    logit_done, logit_ready, aff_exp, aff_ready = sem("logit_done"), sem("logit_ready"), sem("aff_exp"), sem("aff_ready")
    affT_done, slotT_ready, slot_done, slot_ready = sem("affT_done"), sem("slotT_ready"), sem("slot_done"), sem("slot_ready")
    (pick_ready, gathered, pgT_done, x_tok_ready, xgT_done, xg_ready, pgT_ready, w_used, silu_ready, hid_ready,
     hidT_done, hidT_ready,
     y_ready_e, scattered, added, moe_step) = (sem(n) for n in PER_E_NAMES)
    x2_ready = sem("x2_ready")
    s_pos, trig_in, trig_done, s_out = sem("positions_in"), sem("trig_in"), sem("trig_done"), sem("out_written")
    w_seed, oq_done = sem("w_seed"), sem("oq_done")
    uw_done, uw_taken = sem("uw_done"), sem("uw_taken")
    v_done, vnew_ready, sd_done, state_ready, o_done, o_taken = (sem(n) for n in
        ("v_done", "vnew_ready", "sd_done", "state_ready", "o_done", "o_taken"))
    dn_sum, dn_ready = sem("dn_sum"), sem("dn_ready")
    rope_done, rope_turned, rope_taken = sem("rope_in_parts"), sem("rope_turned"), sem("rope_taken")

    N_MODA, N_IN, N_MODB = 4, 6, 8
    IN_CUTS = [(0, 512), (512, 1024), (1024, 1536), (1536, 1808), (1808, 2320), (2320, 2832)]
    chunks = [("mod", i) for i in range(N_MODA)] + [("in", i) for i in range(N_IN)]
    chunks += [("mod", N_MODA + i) for i in range(N_MODB)] + [("dft", 0)]
    FRONT = len(chunks)
    chunks += [("out", 0), ("out", 1)]
    MOE0 = len(chunks)
    EC = 12
    L0 = MOE0 + NE * EC

    def chunk_source(kind, i):
        if kind == "mod":
            return a["w_mod"][:, i * 512:(i + 1) * 512].rearrange("(k p) n -> p k n", p=P)
        if kind == "in":
            lo, hi = IN_CUTS[i]
            return a["w_in"][:, lo:hi].rearrange("(k p) n -> p k n", p=P)
        if kind == "dft":
            return a["dft"].rearrange("c (k p) n -> p (c k) n", p=P)
        if kind == "out":
            return a["w_out"][:, i * 512:(i + 1) * 512].rearrange("(k p) n -> p k n", p=P)

    def freed(n):
        kind, i = chunks[n]
        if kind == "mod":
            return mod_done, i + 1
        if kind == "in":
            return proj_done, sum(g[0] <= i for g in GROUPS)
        if kind == "out":
            return out_done, 4 * i + 4
        return ft_tok_done, 2

    def slot(n, w=512):
        return ring[:, n % SLOTS, 0:8 * w].rearrange("p (k n) -> p k n", k=8)

    GROUPS = []

    def feat(ch, col, dst, i, lat=True, context=False):
        if lat:
            GROUPS.append((ch, "FL", col, dst, i))
        if context:
            GROUPS.append((ch, "FC", col, dst, i))
    for i in range(2):
        feat(0, i * P, q_na, i)
    for i in range(2):
        feat(0, 256 + i * P, k_na, i, context=True)
    for t in range(6):
        GROUPS.append((1, "V", 0, v_na, t))
    for i in range(2):
        feat(1, 256 + i * P, "conv", i)
    for i in range(4):
        feat(2, i * P, "conv", 2 + i, context=True)
    for t in range(6):
        GROUPS.append((3, "AB", 0, ab, t))
    for i in range(2):
        feat(3, 16 + i * P, gate, i)
    for i in range(2):
        feat(4, i * P, q_df, i)
    for i in range(2):
        feat(4, 256 + i * P, k_df, i, context=True)
    for t in range(6):
        GROUPS.append((5, "V", 0, v_df, t))
    for i in range(2):
        feat(5, 256 + i * P, uft, i)
    NG = len(GROUPS)
    IN_W = [hi - lo for lo, hi in IN_CUTS]

    def group_bank(g, kind):
        width = {"FL": T, "FC": L, "V": GW, "AB": 16}[kind]
        return bank[g % 4][:, 0:width]

    def group_dest(kind, dst, i):
        if isinstance(dst, str):
            return cinL[i][:, PAD:PAD + T] if kind == "FL" else cinC[i - 2][:, PAD:PAD + L]
        if kind == "FL":
            return dst[:, i, 0:T]
        if kind == "FC":
            return dst[:, i, T:T + L]
        return dst[:, i, :]

    CONVS = []
    for g, (ch, kind, col, dst, i) in enumerate(GROUPS):
        if dst == "conv":
            to = (dq, dk, dv)[i // 2][:, i % 2, :]
            cin, o = (cinL[i], to[:, 0:T]) if kind == "FL" else (cinC[i - 2], to[:, T:T + L])
            CONVS.append((g, cin, o, i))

    UNITS = [(h, t) for h in range(H) for t in range(TT)]
    NU = len(UNITS)
    KT = ALLT // P
    probsT = region(0, KT, T)
    s_na = [region(3072 + 768 * i, ALLT) for i in range(2)]
    p_na = [region(4608 + 768 * i, ALLT) for i in range(2)]
    p_df = [region(3072 + 1536 * i, 2, ALLT) for i in range(2)]
    score = [ps[i].rearrange("p a b -> p (a b)")[:, 0:ALLT] for i in range(2)]
    tpair = ps[2].rearrange("p a b -> p (a b)")[:, 0:ALLT]
    lam = stat[:, 0:8]

    h2 = region(0, KD, T)
    h_tok = region(4096, TT, D)
    moe_sq = region(8192, KD, T)
    acc = region(8192, KD, T)
    xg = region(12288, KD, CAP)
    sg = [region(12800 + 512 * i, 512) for i in range(2)]
    hid = region(13824, 2, 512)
    hidT = region(14848, 8, P)
    ysb = region(15872, 512)
    pgT = region(16384, T)
    pick = region(16896, TT, CAP)
    pickg = region(17152, TT, 2, CAP)
    moe_r = region(17664, T)
    affT, left, count, zero16 = (region(18176 + 512 * i, T) for i in range(4))
    aff, logit = region(20224, TT, NE), region(20288, TT, NE)
    wr = sb("wr", [P, KD, NE])
    slotE, affE = region(20480, NE + 1, TT), region(20560, NE + 1, TT)
    x_tok = region(20640, 512)
    top8 = stat[0:NE, 48:56]
    _, c2 = later_constants()
    const2 = region(24576, max(hi for lo, hi in c2.values()))
    tab2 = {k: const2[:, lo:hi] for k, (lo, hi) in c2.items()}
    PER_E = dict(pick_ready=1, gathered=1, pgT_done=1, x_tok_ready=1, xgT_done=1, xg_ready=1, pgT_ready=1, w_used=EC, silu_ready=2,
                 hid_ready=2, hidT_done=2, hidT_ready=2, y_ready=1, scattered=8, added=8, moe_step=2)
    SCATTER = (5, 7, 1, 3)

    hT, l_sqb = region(0, KD, T), region(4096, KD, T)
    hidden = region(4096, FT, T)
    qlat, kvlat, ug, vtok = region(4096, 2, T), region(5120, T), region(5632, 2, T), region(6656, TT, GW)
    PW = 16
    pin = region(7680, 2, PW + T)
    kpe = region(8736, T)
    qh, kh, vh = region(9248, H, T), region(11296, H, T), region(13344, TT, H * VH)
    osq = region(9248, KD, T)
    p2 = [region(15392 + 512 * i, T) for i in range(2)]
    pm = region(15392, 2, T)
    pT2 = region(16416, TT, T)
    pools = [region(16416 + 528 * i, PW + T) for i in range(3)]
    R = [region(18464 + 512 * i, T) for i in range(3)]
    rope_c, rope_s = region(26112, T), region(26624, T)
    lsm = region(27136, L_ALL)
    Q = [region(29632 + 512 * i, T) for i in range(3)]
    lpar = lsm[:, 0:L_PAR]
    wq = lsm[:, L_WQ:L_WKV].rearrange("p (i c) -> p i c", i=2)
    wkv = lsm[:, L_WKV:L_WPOOL].rearrange("p (h c) -> p h c", h=H)
    wpool = lsm[:, L_WPOOL:L_WSP].rearrange("p (i c) -> p i c", i=2)
    wsp = lsm[:, L_WSP:L_BSP].rearrange("p (h c) -> p h c", h=H)
    bsp = lsm[:, L_BSP:L_ALL].rearrange("p (i c) -> p i c", i=2)
    Z_W = [416, 512, 256]
    LC = [("in", w) for w in Z_W] + [("out", 512)] * 2 + [("gu", 512)] * 11 + [("down", 0)] * 8
    LAYER_FREED = [("lin_done", 4), ("lin_done", 10), ("lin_done", 12), ("lo_done", 4), ("lo_done", 8)]
    LAYER_FREED += [("up_done", 2 * i + 2) for i in range(11)] + [("down_done", i + 1) for i in range(8)]
    NLC = len(LC)

    def layer_source(l, j):
        kind = LC[j][0]
        if kind == "in":
            lo = sum(Z_W[:j])
            return a["w_in_2"][l, :, lo:lo + Z_W[j]].rearrange("(k p) n -> p k n", p=P)
        if kind == "out":
            return a["w_out_2"][l, :, (j - 3) * 512:(j - 2) * 512].rearrange("(k p) n -> p k n", p=P)
        if kind == "gu":
            return a["w_gu_2"][l, j - 5]
        return a["w_dn_2"][l, j - 16]

    def layer_slot(j):
        s, (kind, w) = ring[:, (L0 + j) % SLOTS, :], LC[j]
        if kind in ("in", "out"):
            return s[:, 0:8 * w].rearrange("p (k n) -> p k n", k=8)
        return s if kind == "gu" else s[:, 0:FF]

    GOES_ON = dict(l_sq=(squares, 42), l_sum=(summed, 14), l_rstd=(rstd_ready, 14), l_h=(h2_ready, KD),
                   lin_done=(proj_done, NG), lin_taken=(proj_taken, NG), sc_done=(score_ready, 48),
                   sc_taken=(na_scores_taken, 16), mx_ready=(na_max_ready, 16), ex_ready=(na_exp_ready, 16),
                   pr_ready=(probs_ready, 32), tr_done=(transposed, 32), pt_taken=(probsT_act, 32),
                   pvl_done=(pv_done, 8), pvl_taken=(pv_taken, 8), lo_done=(out_done, 8), lo_taken=(out_taken, 8),
                   silu_l=(silu_done, len(CONVS) + 1), turned=(rope_turned, 4), roped=(rope_done, 4),
                   l_act=(act_step, 0), l_dve=(dve_step, 0))
    Ls = {n: GOES_ON[n][0] if n in GOES_ON else sem(n) for n in PER_L}
    per_l = {Ls[n].name: k for n, k in PER_L.items()}
    before_l = {s.name: k for s, k in GOES_ON.values()}

    LIN = [(0, "F", 0, qlat[:, 0]), (0, "F", 128, qlat[:, 1]), (0, "F", 256, kvlat), (0, "pe", 384, kpe[64:96]),
           (1, "F", 0, ug[:, 0]), (1, "F", 128, ug[:, 1])]
    LIN += [(1, "V", t, vtok[:, t]) for t in range(TT)]
    LIN += [(2, "F", 128 * i, pin[:, i, PW:PW + T]) for i in range(2)]
    LIN += [(None, "q", h, qh[0:QK_HEAD, h]) for h in range(H)] + [(None, "k", h, kh[0:QK_NOPE, h]) for h in range(H)]
    LIN += [(None, "v", t, vh[:, t]) for t in range(TT)]

    def lin_bank(g):
        kind, b = LIN[g][1], bank[1 + g % 4]
        return {"F": b, "pe": b[64:96], "V": b[:, 0:GW], "q": b[0:QK_HEAD], "k": b[0:QK_NOPE], "v": b}[kind]

    HEADS = [qh[0:QK_HEAD, h] for h in range(H)] + [kh[0:QK_HEAD, h] for h in range(H)]
    turn_bank, head_bank = [bank[6], bank[7]], [bank[0], bank[5]]

    ringf = ring[:].rearrange("p s c -> p (s c)")

    def store(at, *dims):
        v = ringf[:, at:at + int(np.prod(dims))]
        names = "abcde"[:len(dims)]
        return v.rearrange(f"p ({' '.join(names)}) -> p {' '.join(names)}", **dict(zip(names, dims)))

    kdec = store(0, 6, 2, H, CH)
    wT = store(3072, 6, 2, 2, 2, CH)
    uu = store(6144, 6, 2, H, CH)
    qkT = store(9216, TT, 2, H, CH)
    qdec = store(11264, TT, 2, 2, P)
    tokp = store(13312, 7, 6, 8)
    g_, beta, nbeta, gcum, begc, ekd, gl2 = (tokp[:, i] for i in range(7))
    gl2 = gl2.rearrange("p t (c x) -> p t c x", c=2)
    DN_FIELDS = ["gtri", "decay", "nt", "ns", "X", "W", "Y", "vb", "kb", "gb", "eq"]
    dn = [{f: region(5632 * q + 512 * n, 2, H, CH) for n, f in enumerate(DN_FIELDS)} for q in range(2)]
    dn_out = region(11264, 2, 2, T)
    vnew = region(13312, 2, H, CH)
    state = [region(13824 + 256 * i, 2, 2, CH) for i in range(2)]
    PAIRS = [(4, 5), (0, 1), (2, 3)]
    STEPS = 12
    lv_mask = tab["levels"].rearrange("p (s d c) -> p s d c", s=6, d=2)

    def chunk_at(d, i):
        c = (i if d == 0 else 3 - i) if i < 4 else (i - 4 if d == 0 else 11 - i)
        return (4 if i < 4 else 0) + c // 2, c % 2

    l2jobs = [(dq[:, i, :], T) for i in range(2)]
    for i in range(2):
        l2jobs += [(dk[:, i, 0:T], T), (dk[:, i, T:ALLT], L)]
    l2sq = [region(3072 + 512 * i, T) for i in range(6)]
    l2r = [region(6144 + 512 * i, T) for i in range(6)]

    dnA, dnB = [ps[0], ps[1]], [ps[2], ps[3]]
    dnT, dnG = [bank[0], bank[2]], [bank[1], bank[3]]
    dnK = ps[3].rearrange("p o (q m a c) -> p q m a o c", q=2, m=2, a=2)

    def v4(pair):
        return pair[:, :, 0:H * CH].rearrange("p d (h c) -> p d h c", h=H)

    block = ctx.enter_context(nc.Block())

    @block.sync
    def _(sp):
        sp.dma_start(xT[:], a["xT"].rearrange("(k p) n -> p k n", p=P)).then_inc(s_x, 16)
        sp.dma_start(hC, a["ctxT"].rearrange("(k p) n -> p k n", p=P)).then_inc(s_x, 16)
        for n, (kind, i) in enumerate(chunks):
            if n >= SLOTS:
                sp.wait_ge(*freed(n - SLOTS))
            if n == FRONT:
                sp.wait_ge(o_done, 2 * (STEPS - 4))
                sp.wait_ge(state_ready, 1 + 2 * STEPS)
            w = IN_W[i] if kind == "in" else 512
            sp.dma_start(slot(n, w), chunk_source(kind, i)).then_inc(slot_in[n % SLOTS], 16)
        for j in range(EC):
            if 2 <= j < 4:
                sp.wait_ge(out_done, 4 * (j - 1))
            if j >= 4:
                sp.wait_ge(w_used, j - 3)
            sp.dma_start(ring[:, (MOE0 + j) % SLOTS, :], a["w_moe"][0, j]).then_inc(slot_in[(MOE0 + j) % SLOTS], 16)
        with sp.Fori(1, NE) as e:
            for j in range(EC):
                sp.wait_ge(w_used, e * EC + (j - 3))
                sp.dma_start(ring[:, (MOE0 + j) % SLOTS, :], a["w_moe"][bass.ds(e, 1), j].rearrange("a p n -> p (a n)"))\
                  .then_inc(slot_in[(MOE0 + j) % SLOTS], 16)
        for l in range(LAYERS):
            for j in range(NLC):
                if j >= SLOTS:
                    name, k = LAYER_FREED[j - SLOTS]
                    sp.wait_ge(Ls[name], before_l.get(Ls[name].name, 0) + l * PER_L[name] + k)
                elif l == 0:
                    sp.wait_ge(w_used, NE * EC - SLOTS + 1 + j)
                else:
                    name, k = LAYER_FREED[NLC - SLOTS + j]
                    sp.wait_ge(Ls[name], before_l.get(Ls[name].name, 0) + (l - 1) * PER_L[name] + k)
                sp.dma_start(layer_slot(j), layer_source(l, j)).then_inc(slot_in[(L0 + j) % SLOTS], 16)
        for k in range(KD):
            sp.wait_ge(Ls["down_taken"], (LAYERS - 1) * KD + k + 1)
            sp.dma_start(out[k * P:(k + 1) * P], xT[:, k]).then_inc(s_out, 16)
        sp.wait_ge(s_out, 16 * KD)

    @block.gpsimd
    def _(pool):
        pool.memset(condw, 0.0).then_inc(init_done, 1)
        pool.memset(ones[:], 1.0).then_inc(init_done, 1)
        pool.memset(eps[:, 0:1], EPS).then_inc(init_done, 1)
        pool.memset(eps[:, 1:2], 1.0).then_inc(init_done, 1)
        for i in range(6):
            pool.memset(cinL[i], 0.0).then_inc(init_done, 1)
        for i in range(4):
            pool.memset(cinC[i], 0.0).then_inc(init_done, 1)

        pool.wait_ge(conv_done, len(CONVS))
        for h in range(H):
            for half in range(2):
                src = a["rpb"][h, :, 1 - half:15 - half]
                pool.dma_start(rpb[half * 64:half * 64 + 64, h], src).then_inc(s_bias, 16)

        S = Steps(pool)
        for n, pair in enumerate(PAIRS):
            for s in range(6):
                for q, t in enumerate(pair):
                    B = dn[q]
                    if s == 0:
                        pool.wait_ge(nt_ready, 2 * n + q + 1)
                        if n:
                            pool.wait_ge(y_done, 12 * n)
                    else:
                        pool.wait_ge(y_done, 12 * n + 2 * (s - 1) + q + 1)
                    pool.tensor_tensor(B["ns"], B["nt"], spread(lv_mask[:, s], 2, H), ALU.mult).then_inc(ns_ready, 1)

        with pool.Fori(0, LAYERS) as l:
            E = Turn(pool, l, per_l, before_l)
            pool.wait_ge(s_later, 16)
            E.upto(Ls["pad_ready"], 1)
            for i in range(2):
                E.upto(Ls["lin_taken"], 11 + i)
                x, steps = pin[:, i], 2 * i + 2
                for s in range(steps):
                    d = 1 << s
                    lo = 2 * d - 1
                    src = x if s == 0 else pools[(s - 1) % 3]
                    E.mark(pool.tensor_tensor(pools[s % 3][:, lo:], src[:, lo:], src[:, lo - d:PW + T - d], ALU.add), Ls["l_pool"])
                rc = tab2["pool_recip"][:, i * T:(i + 1) * T]
                for o in range(2):
                    half = slice(64 * o, 64 * o + 64)
                    src = pools[(steps - 2 + o) % 3]
                    E.mark(pool.tensor_tensor(pm[half, i], src[half, PW:], rc[half], ALU.mult), Ls["l_pool"])
                E.mark(pool.tensor_tensor(pm[:, i], pm[:, i], x[:, PW:], ALU.subtract), Ls["l_pool" if i == 0 else "pool_ready"])
            for x in HEADS:
                E.wait(Ls["turned"])
                E.mark(pool.tensor_tensor(x, x, rope_c[0:QK_HEAD], ALU.mult), Ls["by_cos"])
            E.end()

    N_INIT = 14

    @block.scalar
    def _(act):
        S = Steps(act)
        act.dma_start(par[:], a["par"]).then_inc(s_par, 16)
        act.dma_start(rows[:], a["rows"].partition_broadcast(P)).then_inc(s_par, 16)

        act.wait_ge(s_par, 32)
        cond = par[:, C_COND:C_COND + 16]
        act.wait_ge(init_done, 1)
        act.activation(condw[:, :, 0:2], cond.rearrange("p (k c) -> p k c", c=2), ACT.Silu).then_inc(cond_ready, 1)

        def copy_mod(n):
            act.wait_ge(mod_done, n + 1)
            if n:
                act.wait_ge(mod_turned, n)
            act.activation(mod_row, bank[6], ACT.Copy).then_inc(mod_copied, 1)

        act.preload_act_table_set(LN_EXP)
        act.wait_ge(s_x, 32)
        for k in range(KD):
            act.activation(sqL[:, k, :], xT[:, k, :], ACT.Square).then_inc(squares, 1)
        for k in range(KD):
            act.activation(sqC[:, k, :], hC[:, k, :], ACT.Square).then_inc(squares, 1)
        act.wait_ge(init_done, N_INIT)
        rstdL, rstdC = region(14336, T), region(14848, L)
        for src, dst in ((bank[4], rstdL), (bank[5][:, 0:L], rstdC)):
            S.wait(summed)
            S.mark(act.activation(dst, src, ACT.Ln, scale=1.0 / D, bias=eps[:, 0:1]), act_step)
            act.activation(dst, dst, ACT.Exp, scale=-0.5).then_inc(rstd_ready, 1)
        for n in range(N_MODA):
            copy_mod(n)
        act.dma_start(ident[:], a["ident"]).then_inc(s_const, 16)
        act.dma_start(const, a["const"]).then_inc(s_const, 16)
        act.dma_start(ftw[:], a["ft_w"].rearrange("(k p) n -> p k n", p=P)).then_inc(s_ftw, 16)
        for k in range(KD):
            for j, h in enumerate((hL, hC)):
                S.wait(scaled)
                act.activation(h[:, k, :], h[:, k, :], ACT.Identity, bias=mod[:, 0, k, j:j + 1]).then_inc(h_ready, 1)
        for g, (ch, kind, col, dst, i) in enumerate(GROUPS):
            S.wait(proj_done)
            act.activation(group_dest(kind, dst, i), group_bank(g, kind), ACT.Copy).then_inc(proj_taken, 1)

        for g, cin, o, i in CONVS:
            S.wait(conv_done)
            act.activation(o, o, ACT.Silu).then_inc(silu_done, 1)

        act.preload_act_table_set(LN_EXP)
        act.wait_ge(lam_ready, 1)
        act.activation(lam[:, 2:4], lam[:, 0:2], ACT.Exp).then_inc(lam_ready, 1)

        def exp_scores(df, u):
            if not df:
                act.wait_ge(na_max_ready, u + 1)
                if u >= 2:
                    act.wait_ge(transposed, u - 1)
                act.activation(p_na[u % 2], s_na[u % 2], ACT.Exp, bias=stat[:, 16 + u % 2:17 + u % 2],
                               accum_out=stat[:, 20 + u % 2:21 + u % 2]).then_inc(na_exp_ready, 1)
                return
            act.wait_ge(transposed, max(NU, NU + u - 1))
            for m in range(2):
                act.wait_ge(df_max_ready, 2 * u + m + 1)
                w = 2 * (u % 2) + m
                act.activation(p_df[u % 2][:, m, :], score[m], ACT.Exp, scale=32 ** -0.5,
                               bias=stat[:, 24 + w:25 + w],
                               accum_out=stat[:, 28 + w:29 + w]).then_inc(df_exp_ready, 1)

        def keep_head(i):
            act.wait_ge(pv_done, i + 1)
            half = slice(64 * (i % 2), 64 * (i % 2) + 64)
            act.activation(mix[half, 4 * (i // H) + i % H // 2, :], bank[6][half, :], ACT.Copy).then_inc(pv_taken, 1)

        for df in range(2):
            exp_scores(df, 0)
            for u, (h, t) in enumerate(UNITS):
                if u + 1 < NU:
                    exp_scores(df, u + 1)
                n = df * NU + u
                if t == 0 and n:
                    keep_head(n // TT - 1)
                act.wait_ge(transposed, n + 1)
                act.activation(probsT[:, 0:4, t * P:(t + 1) * P],
                               tpair[:, 0:512].rearrange("p (k q) -> p k q", k=4), ACT.Copy)\
                   .then_inc(probsT_act, 1)
                if t == 2:
                    copy_mod(N_MODA + n // TT)
        keep_head(2 * H - 1)

        S.at[summed.name] = 2
        dfsq = [region(3072 + 512 * i, T) for i in range(2)]
        dfr = [region(4096 + 512 * i, T) for i in range(2)]
        act.wait_ge(pv_taken, 2 * H)
        for i in range(2):
            act.activation(dfsq[i], mix[:, 4 + i, :], ACT.Square).then_inc(squares, 1)
        for i in range(2):
            S.wait(summed)
            S.mark(act.activation(dfr[i], bank[i], ACT.Ln, scale=1.0 / HD, bias=eps[:, 0:1]), act_step)
            act.activation(dfr[i], dfr[i], ACT.Exp, scale=-0.5).then_inc(rstd_ready, 1)

        ftA, ftY = region(0, TT, 2, 256), region(2048, 2, T)
        for t in range(TT):
            S.wait(ft_chan_done)
            act.activation(ftA[:, t], bank[2 + t % 2].rearrange("p (a b) -> p a b", a=2), ACT.Copy)\
               .then_inc(ft_chan_taken, 1)
        for i in range(2):
            S.wait(ft_tok_done)
            act.activation(ftY[:, i], bank[4 + i], ACT.Copy).then_inc(ft_tok_taken, 1)
        for i in range(2):
            S.wait(ft_done)
            act.activation(mix[:, 6 + i], bank[i], ACT.Copy).then_inc(ft_taken, 1)

        act.wait_ge(silu_done, len(CONVS))
        act.wait_ge(dfo_scaled, 2)
        for sq, (x, n) in zip(l2sq, l2jobs):
            act.activation(sq[:, 0:n], x, ACT.Square).then_inc(squares, 1)
        for j, (r, (x, n)) in enumerate(zip(l2r, l2jobs)):
            S.wait(summed)
            S.mark(act.activation(r[:, 0:n], bank[j][:, 0:n], ACT.Ln, bias=eps[:, 0:1]), act_step)
            act.activation(r[:, 0:n], r[:, 0:n], ACT.Exp, scale=-0.5).then_inc(rstd_ready, 1)
        act.wait_ge(ab_ready, 1)
        act.activation(g_, gcum, ACT.Exp).then_inc(ab_exp, 1)
        act.activation(beta, ab[:, :, 8:16], ACT.Exp, scale=-1.0).then_inc(ab_exp, 1)
        act.activation(rows[:, R_ALOG:R_ALOG + 8], rows[:, R_ALOG:R_ALOG + 8], ACT.Exp).then_inc(ab_exp, 1)
        act.wait_ge(ab_exp, 3)
        act.activation(g_, g_, ACT.Ln, bias=eps[:, 1:2]).then_inc(ab_exp, 1)
        act.wait_ge(gc_ready, 1)
        act.activation(ekd, ekd, ACT.Exp).then_inc(gc_exp, 1)
        act.activation(begc, gcum, ACT.Exp).then_inc(gc_exp, 1)
        for c in range(2):
            for o in range(2):
                half = slice(64 * o, 64 * o + 64)
                act.activation(gl2[half, :, c, :], bank[4 + c][half, o:o + 47:2].rearrange("p (t x) -> p t x", t=6),
                               ACT.Exp).then_inc(gc_exp, 1)

        for n, pair in enumerate(PAIRS):
            for q, t in enumerate(pair):
                S.wait(decay_arg)
                act.activation(dn[q]["decay"], dn[q]["decay"], ACT.Exp).then_inc(decay_ready, 1)
            for q, t in enumerate(pair):
                if t < TT:
                    S.wait(gq_done)
                    act.activation(dn[q]["eq"].rearrange("p a b c -> p (a b c)"), dnG[q], ACT.Exp).then_inc(gq_exp, 1)
            for q, t in enumerate(pair):
                S.wait(w_done)
                act.activation(dn[q]["W"], v4(dnB[q]), ACT.Copy).then_inc(w_seed, 1)
            S.at[w_done.name] += 10
            for q, t in enumerate(pair):
                S.wait(uw_done, 2)
                act.activation(uu[:, t], v4(dnA[q]), ACT.Copy).then_inc(uw_taken, 1)
                for c in range(2):
                    act.activation(wT[:, t, c], dnB[q][:, c, 0:2 * P].rearrange("p (d a x) -> p d a x", d=2, a=2), ACT.Copy)\
                       .then_inc(uw_taken, 1)
        for i in range(4, STEPS):
            for d in range(2):
                t, c = chunk_at(d, i)
                S.wait(o_done)
                act.activation(dn_out[:, d, :, t * P + c * CH:t * P + c * CH + CH],
                               bank[6 + d][:, 0:P].rearrange("p (a b) -> p a b", a=2), ACT.Copy).then_inc(o_taken, 1)
        act.activation(gate, gate, ACT.Silu).then_inc(silu_done, 1)
        act.preload_act_table_set(LN_EXP)
        for i in range(2):
            S.wait(dn_sum)
            act.activation(dn_out[:, 1, i], dn_out[:, 0, i], ACT.Square).then_inc(squares, 1)
        for i in range(2):
            S.wait(summed)
            r = region(512 * i, T)
            S.mark(act.activation(r, bank[i], ACT.Ln, scale=1.0 / HD, bias=eps[:, 0:1]), act_step)
            act.activation(r, r, ACT.Exp, scale=-0.5).then_inc(rstd_ready, 1)

        act.wait_ge(dn_ready, 2)
        act.dma_start(const2, a["const2"]).then_inc(s_later, 16)
        act.dma_start(wr[:], a["w_router"].rearrange("(k p) n -> p k n", p=P)).then_inc(s_wr, 16)

        act.dma_start(region(4096, T).bitcast(I32), a["positions"].partition_broadcast(P)).then_inc(s_pos, 16)
        act.wait_ge(trig_in, 2)
        act.activation(rope_s, rope_s, ACT.Sin).then_inc(trig_done, 1)
        act.activation(rope_c, rope_c, ACT.Sin).then_inc(trig_done, 1)
        act.preload_act_table_set(LN_EXP)

        for k in range(KD):
            S.wait(out_taken)
            act.activation(moe_sq[:, k], xT[:, k], ACT.Square).then_inc(squares, 1)
        S.wait(summed)
        S.mark(act.activation(moe_r, bank[6], ACT.Ln, scale=1.0 / D, bias=eps[:, 0:1]), act_step)
        act.activation(moe_r, moe_r, ACT.Exp, scale=-0.5).then_inc(rstd_ready, 1)
        for k in range(KD):
            S.wait(scaled)
            act.activation(h2[:, k], h2[:, k], ACT.Identity, bias=mod2[:, 1, k:k + 1]).then_inc(h2_ready, 1)
        S.wait(logit_ready)
        act.activation(logit, logit, ACT.Exp).then_inc(aff_exp, 1)
        for n in range(TT * 2):
            t, half = n // 2, n % 2
            S.wait(tok2_done)
            act.activation(h_tok[:, t, half * 512:half * 512 + 512], bank[n % 4], ACT.Copy).then_inc(tok2_taken, 1)

        act.preload_act_table_set(SILU)
        with act.Fori(0, NE) as e:
            E = Turn(act, e, PER_E)
            E.wait(gathered)
            E.sig(act.activation(x_tok, bank[4], ACT.Copy), x_tok_ready)
            E.wait(xgT_done)
            E.sig(act.activation(xg.rearrange("p (s i) c -> p i s c", s=2),
                                 bank[0].rearrange("p (i s c) -> p i s c", i=4, s=2), ACT.Copy), xg_ready)
            E.wait(pgT_done)
            E.sig(act.activation(pgT, bank[6], ACT.Copy), pgT_ready)
            for j in range(2):
                E.upto(w_used, 4 * j + 2)
                E.sig(act.activation(sg[j], bank[j], ACT.Silu), silu_ready)
            for j in range(2):
                E.wait(hidT_done)
                E.sig(act.activation(hidT[:, 4 * j:4 * j + 4], bank[6].rearrange("p (a b) -> p a b", a=4), ACT.Copy), hidT_ready)
            E.upto(w_used, EC)
            E.sig(act.activation(ysb, bank[4], ACT.Copy), y_ready_e)
            E.end()
        act.preload_act_table_set(LN_EXP)
        for k in range(KD):
            act.wait_ge(x2_ready, k + 1)
            act.activation(h2[:, k], xT[:, k], ACT.Square).then_inc(squares, 1)
        S.wait(summed)
        S.mark(act.activation(moe_r, bank[0], ACT.Ln, scale=1.0 / D, bias=eps[:, 0:1]), act_step)
        act.activation(moe_r, moe_r, ACT.Exp, scale=-0.5).then_inc(rstd_ready, 1)

        act.wait_ge(x2_ready, 2 * KD)
        with act.Fori(0, LAYERS) as l:
            act.preload_act_table_set(LN_EXP)
            E = Turn(act, l, per_l, {**before_l, act_step.name: S.at[act_step.name]})
            act.dma_start(lsm, a["small_2"][bass.ds(l, 1)].rearrange("a p n -> p (a n)")).then_inc(Ls["l_in"], 16)

            def squares_of(pairs):
                for dst, src in pairs:
                    E.sig(act.activation(dst, src, ACT.Square), Ls["l_sq"])

            def rstd(dst, src, n):
                E.wait(Ls["l_sum"])
                E.mark(act.activation(dst, src, ACT.Ln, scale=1.0 / n, bias=eps[0:dst.shape[0], 0:1]), Ls["l_act"])
                E.sig(act.activation(dst, dst, ACT.Exp, scale=-0.5), Ls["l_rstd"])

            squares_of([(l_sqb[:, k], xT[:, k]) for k in range(KD)])
            rstd(R[0], bank[0], D)
            for g in range(12):
                E.wait(Ls["lin_done"])
                E.sig(act.activation(LIN[g][3], lin_bank(g), ACT.Copy), Ls["lin_taken"])
            E.upto(Ls["lin_taken"], 12)
            squares_of([(Q[0], qlat[:, 0]), (Q[1], qlat[:, 1]), (Q[2], kvlat)])
            for t in range(TT):
                E.mark(act.activation(qh[:, 0, 0:GW], vtok[:, t], ACT.Square, accum_out=stat[:, t:t + 1]), Ls["l_act"])
            E.mark(act.activation(stat[:, 0:4], stat[:, 0:4], ACT.Ln, scale=1.0 / GW, bias=eps[:, 0:1]), Ls["l_act"])
            E.sig(act.activation(stat[:, 0:4], stat[:, 0:4], ACT.Exp, scale=-0.5), Ls["v_rstd"])
            rstd(R[1], bank[0], 2 * P)
            rstd(R[2], bank[5], P)
            for g in range(12, 24):
                E.wait(Ls["lin_done"])
                E.sig(act.activation(LIN[g][3], lin_bank(g), ACT.Copy), Ls["lin_taken"])
            E.upto(Ls["lin_taken"], 20)
            E.upto(Ls["kpe_ready"], 4)
            for j in range(9):
                if j < 8:
                    if j >= 2:
                        E.upto(Ls["l_rstd"], 3 + j - 1)
                    squares_of([(Q[j % 2][0:QK_HEAD], HEADS[j])])
                if j >= 1:
                    if j >= 3:
                        E.upto(Ls["turn_in"], j - 2)
                    rstd(R[(j - 1) % 2][0:QK_HEAD], head_bank[(j - 1) % 2][0:QK_HEAD], QK_HEAD)

            def exps(u):
                n = (UNITS[u][1] + 1) * P
                E.upto(Ls["mx_ready"], u + 1)
                if u >= 2:
                    E.upto(Ls["tr_done"], u - 1)
                E.sig(act.activation(p2[u % 2][:, 0:n], p2[u % 2][:, 0:n], ACT.Exp, bias=stat[:, 16 + u % 2:17 + u % 2],
                                     accum_out=stat[:, 20 + u % 2:21 + u % 2]), Ls["ex_ready"])
            def keep_head(h):
                E.wait(Ls["pvl_done"])
                E.sig(act.activation(mix[:, h], bank[4], ACT.Copy), Ls["pvl_taken"])

            exps(0)
            for u, (h, t) in enumerate(UNITS):
                if u + 1 < NU:
                    exps(u + 1)
                if t == 0 and h:
                    keep_head(h - 1)
                E.upto(Ls["tr_done"], u + 1)
                E.sig(act.activation(pT2[:, 0:t + 1, t * P:(t + 1) * P],
                                     bank[3][:, 0:(t + 1) * P].rearrange("p (k q) -> p k q", q=P), ACT.Copy), Ls["pt_taken"])
            keep_head(H - 1)
            E.upto(Ls["pvl_taken"], 4)
            E.upto(Ls["pool_taken"], 2)
            squares_of([(osq[:, k], mix[:, k]) for k in range(KD)])
            for i, (b, n) in enumerate(((0, 512), (5, 256), (6, 256))):
                rstd(R[i], bank[b], n)
            for k in range(KD):
                E.wait(Ls["lo_taken"])
                squares_of([(l_sqb[:, k], xT[:, k])])
            rstd(R[0], bank[0], D)
            act.preload_act_table_set(SILU)
            for f in range(FT):
                E.wait(Ls["gate_done"])
                if f >= 2:
                    E.upto(Ls["hidden"], f - 1)
                E.sig(act.activation(p2[f % 2], bank[f % 2], ACT.Silu), Ls["silu_l"])
            E.upto(Ls["down_taken"], KD)
            E.end()

    @block.vector
    def _(dve):
        S = Steps(dve)
        dve.wait_ge(s_par, 32)
        S.wait(mod_turned, 4)
        src = bank[7][:, 0:32].rearrange("p (s k c) -> p s k c", s=2, c=2)
        bm = par[:, C_BMOD:C_BMOD + 16].rearrange("p (s k) -> p s k", s=2)
        S.mark(dve.tensor_tensor(mod[:], src, spread(bm, 3, 2), ALU.add), mod_taken)
        S.mark(dve.tensor_scalar(gscale[:], mod[:, 1], 1.0, None, ALU.add), dve_step)
        S.mark(dve.tensor_tensor(gscale[:], gscale[:], spread(par[:, C_N1:C_N1 + KD], 2, 2), ALU.mult), dve_step)
        rstdL, rstdC = region(14336, T), region(14848, L)
        S.wait(rstd_ready, 2)
        for k in range(KD):
            for j, (src, h, r) in enumerate(((xT, hL, rstdL), (hC, hC, rstdC))):
                dve.scalar_tensor_tensor(h[:, k, :], src[:, k, :], gscale[:, k, j:j + 1], r, ALU.mult, ALU.mult)\
                   .then_inc(scaled, 1)

        lq = rows[:, R_LAM:R_LAM + 128].rearrange("p (a b c) -> p a b c", a=2, b=2)
        prod = lq[:, :, 0]
        S.mark(dve.tensor_tensor(prod, lq[:, :, 0], lq[:, :, 1], ALU.mult), dve_step)
        dve.tensor_reduce(lam[:, 0:2], prod, AX_X, ALU.add).then_inc(lam_ready, 1)

        for g, cin, o, i in CONVS:
            dve.wait_ge(proj_taken, g + 1)
            n = o.shape[1]
            w = par[:, C_CONV + 5 * i:C_CONV + 5 * i + 5]
            S.mark(dve.tensor_scalar(o, cin[:, 0:n], w[:, 0:1], None, ALU.mult), dve_step)
            for k in range(1, CONV):
                S.mark(dve.scalar_tensor_tensor(o, cin[:, k:k + n], w[:, k:k + 1], o, ALU.mult, ALU.add),
                       conv_done if k == CONV - 1 else dve_step)

        dve.wait_ge(lam_ready, 2)
        S.mark(dve.tensor_tensor(lam[:, 4:5], lam[:, 3:4], lam[:, 2:3], ALU.subtract), dve_step)
        S.mark(dve.tensor_scalar(lam[:, 5:6], lam[:, 4:5], -LAM_INIT, None, ALU.add), dve_step)
        nlam = lam[:, 5:6]

        dve.wait_ge(s_const, 32)
        dve.wait_ge(proj_taken, NG)
        for n, x in enumerate([q_df[:, 0], q_df[:, 1], k_df[:, 0, 0:T], k_df[:, 1, 0:T]]):
            dve.wait_ge(rope_turned, n + 1)
            t1 = region(3072 + 512 * (n % 2), T)
            S.mark(dve.tensor_tensor(t1, bank[n % 2], tab["rope_sin"], ALU.mult), rope_taken)
            S.mark(dve.tensor_tensor(x, x, tab["rope_cos"], ALU.mult), dve_step)
            S.mark(dve.tensor_tensor(x, x, t1, ALU.add), rope_done)

        dve.wait_ge(s_bias, 16 * 2 * H)
        S.mark(dve.tensor_tensor(rpb.rearrange("p h j c -> p (h j) c"), rpb.rearrange("p h j c -> p (h j) c"),
                                 spread(tab["na_mask"], 1, H * 14), ALU.add), dve_step)

        def na_front(u):
            h, t = UNITS[u]
            s = s_na[u % 2]
            dve.wait_ge(score_ready, u + 1)
            if u >= 2:
                dve.wait_ge(na_exp_ready, u - 1)
            rows_ = rpb[:, h, 6 - 2 * t:14 - 2 * t, :].rearrange("p j c -> p (j c)")
            S.mark(dve.scalar_tensor_tensor(s[:, 0:T], score[u % 2][:, 0:T], HD ** -0.5, rows_, ALU.mult, ALU.add), dve_step)
            S.mark(dve.tensor_scalar(s[:, T:ALLT], score[u % 2][:, T:ALLT], HD ** -0.5, None, ALU.mult), na_scores_taken)
            S.mark(dve.tensor_reduce(stat[:, 18 + u % 2:19 + u % 2], s, AX_X, ALU.max), dve_step)
            dve.tensor_scalar(stat[:, 16 + u % 2:17 + u % 2], stat[:, 18 + u % 2:19 + u % 2], -1.0, None, ALU.mult)\
               .then_inc(na_max_ready, 1)

        def df_front(u):
            for m in range(2):
                w = 2 * (u % 2) + m
                dve.wait_ge(score_ready, NU + 2 * u + m + 1)
                S.mark(dve.tensor_reduce(stat[:, 32 + m:33 + m], score[m], AX_X, ALU.max), dve_step)
                if u >= 2:
                    dve.wait_ge(df_exp_ready, 2 * (u - 1))
                dve.tensor_scalar(stat[:, 24 + w:25 + w], stat[:, 32 + m:33 + m], -(32 ** -0.5), None, ALU.mult)\
                   .then_inc(df_max_ready, 1)

        def na_norm(u):
            dve.wait_ge(na_exp_ready, u + 1)
            S.mark(dve.reciprocal(stat[:, 22:23], stat[:, 20 + u % 2:21 + u % 2]), dve_step)
            S.mark(dve.tensor_scalar(p_na[u % 2], p_na[u % 2], stat[:, 22:23], None, ALU.mult), probs_ready)

        def df_norm(u):
            p, w = p_df[u % 2], 2 * (u % 2)
            dve.wait_ge(df_exp_ready, 2 * u + 2)
            S.mark(dve.reciprocal(stat[:, 36:38], stat[:, 28 + w:30 + w]), dve_step)
            S.mark(dve.tensor_scalar(p[:, 1], p[:, 1], stat[:, 37:38], nlam, ALU.mult, ALU.mult), dve_step)
            S.mark(dve.scalar_tensor_tensor(p[:, 0], p[:, 0], stat[:, 36:37], p[:, 1], ALU.mult, ALU.add), probs_ready)

        for df, front, norm in ((0, na_front, na_norm), (1, df_front, df_norm)):
            front(0)
            for u, (h, t) in enumerate(UNITS):
                n = df * NU + u
                if df:
                    norm(u)
                if u + 1 < NU:
                    front(u + 1)
                if not df:
                    norm(u)
                dve.wait_ge(transposed, n + 1)
                if t == 0 and n > 0:
                    dve.wait_ge(pv_done, n // TT)
                S.mark(dve.tensor_copy(probsT[:, 4:6, t * P:(t + 1) * P],
                                       tpair[:, 512:768].rearrange("p (k q) -> p k q", k=2)), probsT_dve)

        dve.wait_ge(mod_turned, N_MODA + N_MODB)
        S.mark(dve.tensor_tensor(mod2[:], bank[7][:, 32:64].rearrange("p (a b) -> p a b", a=4),
                                 par[:, C_BMOD + 16:C_BMOD + 48].rearrange("p (a b) -> p a b", a=4), ALU.add), mod_taken)

        dfr = [region(4096 + 512 * i, T) for i in range(2)]
        S.mark(dve.tensor_scalar(stat[:, 40:41], par[:, C_DFG:C_DFG + 1], 1.0 - LAM_INIT, None, ALU.mult), dve_step)
        for i in range(2):
            S.wait(rstd_ready)
            S.mark(dve.scalar_tensor_tensor(mix[:, 4 + i], mix[:, 4 + i], stat[:, 40:41], dfr[i], ALU.mult, ALU.mult), dfo_scaled)

        dve.wait_ge(ft_tok_done, 2)
        a_in = ab[:, :, 0:8]
        S.mark(dve.tensor_tensor(a_in, a_in, spread(rows[:, R_DT:R_DT + 8], 1, 6), ALU.add), dve_step)
        S.mark(dve.scalar_tensor_tensor(gcum, a_in, -1.0, a_in, ALU.mult, ALU.min), ab_ready)
        for j, (r, (x, n)) in enumerate(zip(l2r, l2jobs)):
            S.wait(rstd_ready)
            S.mark(dve.scalar_tensor_tensor(x, x, HD ** -0.5 if j < 2 else 1.0, r[:, 0:n], ALU.mult, ALU.mult), normed)
        S.wait(ab_exp, 4)
        S.mark(dve.scalar_tensor_tensor(g_, a_in, 0.0, g_, ALU.max, ALU.add), dve_step)
        S.mark(dve.scalar_tensor_tensor(g_, g_, -1.0, spread(rows[:, R_ALOG:R_ALOG + 8], 1, 6), ALU.mult, ALU.mult),
               g_ready)
        S.mark(dve.tensor_scalar(beta, beta, 1.0, None, ALU.add), dve_step)
        S.mark(dve.reciprocal(beta, beta), dve_step)
        S.mark(dve.tensor_scalar(nbeta, beta, -1.0, None, ALU.mult), dve_step)
        S.wait(gc_done)
        for d in range(2):
            src = bank[6][:, 48 * d:48 * d + 48].rearrange("p (t x) -> p t x", t=6)[:, :, 4 * d:4 * d + 4]
            S.mark(dve.tensor_copy(gcum[:, :, 4 * d:4 * d + 4], src), dve_step)
        S.mark(dve.tensor_tensor(ekd, bank[6][:, 96:144].rearrange("p (t x) -> p t x", t=6), gcum, ALU.subtract), gc_ready)
        S.wait(gc_exp, 6)
        S.mark(dve.tensor_tensor(begc, begc, beta, ALU.mult), dn_coef)

        def per_token(x, t):
            return spread(x[:, t].rearrange("p (d h) -> p d h", d=2), 3, CH)

        tri64 = tab["tri64"].rearrange("p (d c) -> p d c", d=2)
        incl = tab["incl"].rearrange("p (d c) -> p d c", d=2)
        for n, pair in enumerate(PAIRS):
            for q, t in enumerate(pair):
                B = dn[q]
                S.mark(dve.tensor_tensor(B["gtri"], spread(tri64, 2, H), per_token(g_, t), ALU.mult), gtri_ready)
                if t < TT:
                    S.mark(dve.tensor_copy(B["gb"], per_token(g_, t)), gb_ready)
            for q, t in enumerate(pair):
                B = dn[q]
                S.wait(tok_done)
                kt = spread(dnT[q][:, 0:GW].rearrange("p (h c) -> p h c", h=H), 1, 2)
                vt = spread(dnT[q][:, GW:2 * GW].rearrange("p (h c) -> p h c", h=H), 1, 2)
                S.mark(dve.tensor_tensor(B["kb"], kt, per_token(begc, t), ALU.mult), dve_step)
                S.mark(dve.tensor_tensor(kdec[:, t], kt, per_token(ekd, t), ALU.mult), dve_step)
                S.mark(dve.tensor_tensor(B["vb"], vt, per_token(beta, t), ALU.mult), tok_taken)
            for q, t in enumerate(pair):
                B = dn[q]
                S.wait(grow_done)
                S.mark(dve.tensor_tensor(B["decay"], dnG[q].rearrange("p (d h c) -> p d h c", d=2, h=H), per_token(gcum, t), ALU.subtract), dve_step)
                S.mark(dve.tensor_tensor(B["decay"], B["decay"], spread(incl, 2, H), ALU.add), decay_arg)
            for q, t in enumerate(pair):
                B = dn[q]
                S.wait(decay_ready)
                S.wait(kk_done, 2 if q == 0 else 0)
                for m, to in enumerate((B["nt"], qkT[:, t]) if t < TT else (B["nt"],)):
                    for d in range(2):
                        S.mark(dve.tensor_tensor(to[:, d].rearrange("p (a o) c -> p a o c", o=2), dnK[:, q, m],
                                                 B["decay"][:, d].rearrange("p (a o) c -> p a o c", o=2), ALU.mult),
                               dve_step if d == 0 else (nt_ready, qk_ready)[m])
            for q, t in enumerate(pair):
                if t < TT:
                    S.wait(gq_exp)
                    qx = spread(dq[:, :, t * P:(t + 1) * P], 1, 2)
                    S.mark(dve.tensor_tensor(qdec[:, t], qx, dn[q]["eq"].rearrange("p a b c -> p (a b c)").rearrange(
                        "p (d a c) -> p d a c", d=2, a=2), ALU.mult), dve_step)
            for s in range(6):
                for q, t in enumerate(pair):
                    B = dn[q]
                    S.wait(y_done)
                    S.mark(dve.tensor_tensor(B["Y"], v4(dnA[q]), per_token(nbeta, t), ALU.mult), dve_step if s == 0 else y_ready)
                    if s == 0:
                        eye = spread(spread(tab["eye64"], 1, H), 1, 2)
                        S.mark(dve.tensor_tensor(B["X"], B["Y"], eye, ALU.add), x_ready)
                if s == 0:
                    continue
                for q, t in enumerate(pair):
                    B = dn[q]
                    if s < 5:
                        S.wait(x_done)
                        S.mark(dve.tensor_tensor(B["X"], B["X"], v4(dnA[q]), ALU.add), x_ready)
                    if s == 1:
                        S.at[w_done.name] = S.at.get(w_done.name, 0) + (2 if q == 0 else 0)
                        S.wait(w_seed)
                    S.wait(w_done)
                    S.mark(dve.tensor_tensor(B["W"], B["W"], v4(dnB[q]), ALU.add), w_ready)

        S.mark(dve.memset(state[0], 0.0), state_ready)
        dve.wait_ge(uw_taken, 6 * len(PAIRS))
        for i in range(STEPS):
            at = [chunk_at(d, i) for d in range(2)]
            halves = [slice(64 * c, 64 * c + 64) for t, c in at]
            for d, (t, c) in enumerate(at):
                S.wait(v_done)
                if i > 4:
                    dve.wait_ge(o_done, 2 * (i - 5) + d + 1)
                r = halves[d]
                v = ps[d][r, :, 0:P].rearrange("p o (a c) -> p o a c", a=2)
                by_bank = "p (a o) c -> p o a c"
                S.mark(dve.tensor_tensor(vnew[r, d].rearrange(by_bank, o=2), uu[r, t, d].rearrange(by_bank, o=2), v,
                                         ALU.subtract), vnew_ready)
            for d, (t, c) in enumerate(at):
                old, new = state[i % 2], state[(i + 1) % 2]
                S.mark(dve.tensor_tensor(new[:, d], old[:, d], spread(gl2[:, t, c, 2 * d:2 * d + 2], 2, CH), ALU.mult), dve_step)
                S.wait(sd_done)
                S.mark(dve.tensor_tensor(new[:, d], new[:, d], bank[4 + d][:, 0:P].rearrange("p (a b) -> p a b", a=2), ALU.add),
                       state_ready)
        for i in range(2):
            dve.wait_ge(o_taken, 2 * (STEPS - 4))
            S.mark(dve.tensor_tensor(dn_out[:, 0, i], dn_out[:, 0, i], dn_out[:, 1, i], ALU.add), dn_sum)
        for i in range(2):
            S.wait(rstd_ready)
            r, y = region(512 * i, T), mix[:, 2 + i]
            dve.wait_ge(silu_done, len(CONVS) + 1)
            S.mark(dve.scalar_tensor_tensor(y, dn_out[:, 0, i], par[:, C_DNG:C_DNG + 1], r, ALU.mult, ALU.mult), dve_step)
            S.mark(dve.tensor_tensor(y, y, gate[:, i], ALU.mult), dn_ready)

        pos, ang, turns = region(4096, T).bitcast(I32), region(4608, T), region(5120, T)
        dve.wait_ge(s_pos, 16)
        dve.wait_ge(s_later, 16)
        S.mark(dve.tensor_copy(ang, pos), dve_step)
        S.mark(dve.tensor_scalar(ang, ang, tab2["inv_freq"], None, ALU.mult), dve_step)
        for dst, quarter in ((rope_s, 0.0), (rope_c, 0.25)):
            S.mark(dve.tensor_scalar(turns, ang, 1.0 / (2 * np.pi), quarter, ALU.mult, ALU.add), dve_step)
            S.mark(dve.tensor_scalar(turns, turns, 12582912.0, None, ALU.add), dve_step)
            S.mark(dve.tensor_scalar(turns, turns, -12582912.0, None, ALU.add), dve_step)
            for i, part in enumerate(TWO_PI):
                S.mark(dve.scalar_tensor_tensor(dst, turns, -part, ang if i == 0 else dst, ALU.mult, ALU.add), dve_step)
            S.mark(dve.tensor_scalar(dst, dst, 2 * np.pi * quarter, None, ALU.add), dve_step)
            S.mark(dve.tensor_scalar(dst, dst, 3.1415925, -3.1415925, ALU.min, ALU.max), trig_in)

        for n in range(KD):
            S.wait(out_done)
            S.mark(dve.scalar_tensor_tensor(xT[:, n], bank[2 + n % 4], mod2[:, 0, n:n + 1], xT[:, n], ALU.mult, ALU.add),
                   out_taken)
        gs2 = gscale[:, :, 0]
        S.mark(dve.tensor_scalar(gs2, mod2[:, 2], 1.0, None, ALU.add), dve_step)
        S.mark(dve.tensor_tensor(gs2, gs2, par[:, C_N2:C_N2 + KD], ALU.mult), dve_step)
        S.wait(rstd_ready)
        for k in range(KD):
            dve.scalar_tensor_tensor(h2[:, k], xT[:, k], gscale[:, k, 0:1], moe_r, ALU.mult, ALU.mult).then_inc(scaled, 1)
        m4 = stat[:, 42:46]
        S.wait(logit_done)
        src = bank[7][:, 0:TT * NE].rearrange("p (t e) -> p t e", t=TT)
        S.mark(dve.tensor_reduce(m4, src, AX_X, ALU.max), dve_step)
        S.mark(dve.tensor_tensor(logit, src, spread(m4, 2, NE), ALU.subtract), logit_ready)
        S.wait(aff_exp)
        S.mark(dve.tensor_reduce(m4, logit, AX_X, ALU.add), dve_step)
        S.mark(dve.reciprocal(m4, m4), dve_step)
        S.mark(dve.tensor_tensor(aff, logit, spread(m4, 2, NE), ALU.mult), aff_ready)
        S.mark(dve.memset(affE[:, NE], 0.0), dve_step)
        S.mark(dve.memset(slotE[:, NE], 0.0), dve_step)
        S.mark(dve.tensor_copy(affE[:, 0:NE], aff.rearrange("p t e -> p e t")), dve_step)
        S.wait(affT_done)
        S.mark(dve.tensor_copy(affT[0:NE], bank[6][0:NE]), dve_step)
        S.mark(dve.tensor_copy(left[0:NE], affT[0:NE]), dve_step)
        S.mark(dve.memset(zero16[0:NE], 0.0), dve_step)
        for _ in range(CAP // 8):
            S.mark(dve.max(top8, left[0:NE]), dve_step)
            S.mark(dve.match_replace(left[0:NE], top8, left[0:NE], -1.0), dve_step)
        S.mark(dve.tensor_tensor(left[0:NE], left[0:NE], affT[0:NE], ALU.not_equal), dve_step)
        S.mark(dve.tensor_tensor_scan(count[0:NE], left[0:NE], zero16[0:NE], 0.0, ALU.add, ALU.add), dve_step)
        S.mark(dve.tensor_tensor(count[0:NE], count[0:NE], left[0:NE], ALU.mult), dve_step)
        S.mark(dve.tensor_scalar(count[0:NE], count[0:NE], -1.0, None, ALU.add), slotT_ready)
        S.wait(slot_done)
        S.mark(dve.tensor_copy(slotE[:, 0:NE], bank[7][:, 0:TT * NE].rearrange("p (t e) -> p e t", t=TT)), slot_ready)
        dve.wait_ge(s_later, 16)

        def choose(mark, se, ae):
            se, ae = (spread(v.rearrange("p a t -> p (a t)"), 2, CAP) for v in (se, ae))
            mark(dve.tensor_tensor(pick, spread(tab2["iota"], 1, TT), se, ALU.is_equal), False)
            mark(dve.tensor_tensor(pickg[:, :, 0], pick, ae, ALU.mult), False)
            mark(dve.tensor_copy(pickg[:, :, 1], pickg[:, :, 0]), True)

        choose(lambda i, last: S.mark(i, pick_ready if last else dve_step), slotE[:, 0:1], affE[:, 0:1])
        S.mark(dve.memset(acc, 0.0), added)
        with dve.Fori(0, NE) as e:
            E = Turn(dve, e, PER_E, {pick_ready.name: 1, added.name: 1})
            for j in range(2):
                E.wait(silu_ready)
                E.upto(w_used, 4 * j + 4)
                E.mark(dve.tensor_tensor(hid[:, j], sg[j], bank[2 + j], ALU.mult), hid_ready)
            E.wait(pgT_done)
            choose(lambda i, last: E.mark(i, pick_ready if last else moe_step),
                   slotE[:, bass.ds(e + 1, 1), :], affE[:, bass.ds(e + 1, 1), :])
            for n in range(KD):
                dt = 4 * (n % 2) + n // 2
                E.wait(scattered)
                E.mark(dve.tensor_tensor(acc[:, dt], acc[:, dt], bank[SCATTER[n % 4]], ALU.add), added)
            E.end()
        for k in range(KD):
            S.mark(dve.scalar_tensor_tensor(xT[:, k], acc[:, k], mod2[:, 3, k:k + 1], xT[:, k], ALU.mult, ALU.add), x2_ready)
        S.wait(rstd_ready)
        for k in range(KD):
            S.mark(dve.scalar_tensor_tensor(xT[:, k], xT[:, k], par[:, C_NF + k:C_NF + k + 1], moe_r, ALU.mult, ALU.mult), x2_ready)

        S.wait(trig_done, 2)

        with dve.Fori(0, LAYERS) as l:
            E = Turn(dve, l, per_l, {**before_l, dve_step.name: S.at[dve_step.name]})
            step = Ls["l_dve"]

            def scaled_norm(x, gain, r, s):
                E.mark(dve.scalar_tensor_tensor(x[1], x[0], gain, r, ALU.mult, ALU.mult), Ls[s])

            E.upto(Ls["l_in"], 16)
            E.mark(dve.tensor_tensor(wsp, wsp, spread(tab2["keep"], 1, H), ALU.mult), Ls["wsp_ready"])
            E.wait(Ls["l_rstd"])
            for k in range(KD):
                scaled_norm((xT[:, k], hT[:, k]), lpar[:, k:k + 1], R[0], "l_h")
            E.mark(dve.memset(pin[:, :, 0:PW], 0.0), Ls["pad_ready"])
            E.wait(Ls["v_rstd"])
            for t in range(TT):
                E.mark(dve.tensor_scalar(vtok[:, t], vtok[:, t], stat[:, t:t + 1], None, ALU.mult), Ls["v_scaled"])
            E.wait(Ls["l_rstd"], 2)
            for i, x in enumerate((qlat[:, 0], qlat[:, 1], kvlat)):
                scaled_norm((x, x), lpar[:, 24 + i:25 + i], R[1 + i // 2], "qn_ready")
            for h in range(H):
                E.mark(dve.tensor_copy(kh[64:96, h], kpe[64:96]), Ls["kpe_ready"])
            for i in range(2):
                E.wait(Ls["sgu_done"])
                y = mix[:, 4 + i]
                E.mark(dve.scalar_tensor_tensor(y.rearrange("p (t c) -> p t c", t=TT), bank[5 + i].rearrange("p (t c) -> p t c", t=TT),
                                                lpar[:, 27 + i:28 + i], spread(bsp[:, i], 1, TT), ALU.mult, ALU.add), step)
                E.mark(dve.tensor_tensor(y, y, ug[:, i], ALU.mult), step)
            for i in range(2):
                E.wait(Ls["pool_done"])
                E.mark(dve.tensor_scalar(mix[:, 6 + i], bank[(7, 0)[i]], lpar[:, 29 + i:30 + i], None, ALU.mult), Ls["pool_taken"])
            def rotate(j):
                x = HEADS[j]
                E.wait(Ls["turned"])
                t = Q[2][0:QK_HEAD]
                E.mark(dve.tensor_tensor(t, turn_bank[j % 2][0:QK_HEAD], rope_s[0:QK_HEAD], ALU.mult), step)
                E.wait(Ls["by_cos"])
                E.mark(dve.tensor_tensor(x, x, t, ALU.add), Ls["roped"])
            for j in range(8):
                E.wait(Ls["l_rstd"])
                scaled_norm((HEADS[j], HEADS[j]), lpar[0:QK_HEAD, 31 + j // 4:32 + j // 4], R[j % 2][0:QK_HEAD], "turn_in")
                if j:
                    rotate(j - 1)
            rotate(7)

            def front(u):
                n, s = (UNITS[u][1] + 1) * P, p2[u % 2]
                E.upto(Ls["sc_done"], u + 1)
                if u >= 2:
                    E.upto(Ls["tr_done"], u - 1)
                b, sc = bank[1 + u % 2], QK_HEAD ** -0.5
                if n > P:
                    E.mark(dve.tensor_scalar(s[:, 0:n - P], b[:, 0:n - P], sc, None, ALU.mult), step)
                E.mark(dve.scalar_tensor_tensor(s[:, n - P:n], b[:, n - P:n], sc, tab2["causal"], ALU.mult, ALU.add), Ls["sc_taken"])
                E.mark(dve.tensor_reduce(stat[:, 18 + u % 2:19 + u % 2], s[:, 0:n], AX_X, ALU.max), step)
                E.mark(dve.tensor_scalar(stat[:, 16 + u % 2:17 + u % 2], stat[:, 18 + u % 2:19 + u % 2], -1.0, None, ALU.mult),
                       Ls["mx_ready"])
            front(0)
            for u, (h, t) in enumerate(UNITS):
                if u + 1 < NU:
                    front(u + 1)
                E.upto(Ls["ex_ready"], u + 1)
                E.mark(dve.reciprocal(stat[:, 22:23], stat[:, 20 + u % 2:21 + u % 2]), step)
                s = p2[u % 2][:, 0:(t + 1) * P]
                E.mark(dve.tensor_scalar(s, s, stat[:, 22:23], None, ALU.mult), Ls["pr_ready"])
            for k in range(KD):
                if k in (0, 4, 6):
                    E.wait(Ls["l_rstd"])
                scaled_norm((mix[:, k], mix[:, k]), lpar[:, 16 + k:17 + k], R[(0, 0, 0, 0, 1, 1, 2, 2)[k]], "mixn")
            for k in range(KD):
                E.wait(Ls["lo_done"])
                E.mark(dve.tensor_tensor(xT[:, k], xT[:, k], bank[1 + k % 4], ALU.add), Ls["lo_taken"])
            E.wait(Ls["l_rstd"])
            for k in range(KD):
                scaled_norm((xT[:, k], hT[:, k]), lpar[:, 8 + k:9 + k], R[0], "l_h")
            for f in range(FT):
                E.wait(Ls["silu_l"])
                E.wait(Ls["up_done"])
                E.mark(dve.tensor_tensor(hidden[:, f], p2[f % 2], bank[2 + f % 2], ALU.mult), Ls["hidden"])
            for k in range(KD):
                E.wait(Ls["down_done"])
                E.mark(dve.tensor_tensor(xT[:, k], xT[:, k], bank[4 + k % 2], ALU.add), Ls["down_taken"])
            E.end()

    @block.tensor
    def _(pe):
        S = Steps(pe)

        def arrived(n):
            pe.wait_ge(slot_in[n % SLOTS], 16 * (n // SLOTS + 1))

        pe.wait_ge(init_done, N_INIT)
        for dst, sq in ((bank[4], sqL), (bank[5][:, 0:L], sqC)):
            for k in range(KD):
                S.wait(squares)
                mm = pe.matmul(dst, ones[:], sq[:, k, :], start=(k == 0), stop=(k == KD - 1))
            mm.then_inc(summed, 1)
        pe.wait_ge(cond_ready, 1)

        def mod_sums(w):
            for r in range(2):
                for g in range(4):
                    k = 4 * r + g
                    mm = pe.matmul(bank[6][32 * g:32 * g + 32], condw[:, k], w[:, k], start=(r == 0), stop=(r == 1))
            mm.then_inc(mod_done, 1)

        for n in range(N_MODA):
            arrived(n)
            mod_sums(slot(n))
            pe.wait_ge(mod_copied, n + 1)
            for j in range(4):
                at = 2 * (4 * n + j)
                mm = pe.matmul(bank[7][:, at:at + 2], mod_row[:, j * P:(j + 1) * P], cond_sel, start=True, stop=True)
            mm.then_inc(mod_turned, 1)
        n0, last = N_MODA, None
        for g, (ch, kind, col, dst, i) in enumerate(GROUPS):
            if ch != last:
                arrived(n0 + ch)
                last = ch
            if g >= 4:
                pe.wait_ge(proj_taken, g - 3)
            w = slot(n0 + ch, IN_W[ch])
            dstp = group_bank(g, kind)
            for k in range(KD):
                se = dict(start=(k == 0), stop=(k == KD - 1))
                if g == 0:
                    S.wait(h_ready, 2)
                if kind == "FL":
                    mm = pe.matmul(dstp, w[:, k, col:col + P], hL[:, k, :], **se)
                elif kind == "FC":
                    mm = pe.matmul(dstp, w[:, k, col:col + P], hC[:, k, :], **se)
                else:
                    h = hL[:, k, i * P:(i + 1) * P] if i < TT else hC[:, k, (i - TT) * P:(i - TT + 1) * P]
                    mm = pe.matmul(dstp, h, w[:, k, col:col + dstp.shape[1]], **se)
            mm.then_inc(proj_done, 1)

        pe.wait_ge(proj_taken, NG)
        pe.wait_ge(s_const, 32)
        for n, x in enumerate([q_df[:, 0], q_df[:, 1], k_df[:, 0, 0:T], k_df[:, 1, 0:T]]):
            if n >= 2:
                pe.wait_ge(rope_taken, n - 1)
            pe.matmul(bank[n % 2], tab["rope_turn"], x, start=True, stop=True).then_inc(rope_turned, 1)
        pe.wait_ge(rope_done, 4)

        def na_scores(u):
            h, t = UNITS[u]
            r = slice(64 * (h % 2), 64 * (h % 2) + 64)
            if u >= 2:
                pe.wait_ge(na_scores_taken, u - 1)
            q = q_na[r, h // 2, t * P:(t + 1) * P]
            pe.matmul(score[u % 2][:, 0:T], q, k_na[r, h // 2, 0:T], start=True, stop=True)
            pe.matmul(score[u % 2][:, T:ALLT], q, k_na[r, h // 2, T:ALLT], start=True, stop=True)\
              .then_inc(score_ready, 1)

        def df_scores(u):
            h, t = UNITS[u]
            for m in range(2):
                lo = 64 * (h % 2) + 32 * m
                r = slice(lo, lo + 32)
                if u >= 1:
                    pe.wait_ge(df_exp_ready, 2 * (u - 1) + m + 1)
                else:
                    pe.wait_ge(na_scores_taken, NU)
                q = q_df[r, h // 2, t * P:(t + 1) * P]
                pe.matmul(score[m][:, 0:T], q, k_df[r, h // 2, 0:T], start=True, stop=True)
                pe.matmul(score[m][:, T:ALLT], q, k_df[r, h // 2, T:ALLT], start=True, stop=True)\
                  .then_inc(score_ready, 1)

        def weighted(i):
            v, h = (v_na, v_df)[i // H], i % H
            pe.wait_ge(probsT_act, TT * (i + 1))
            pe.wait_ge(probsT_dve, TT * (i + 1))
            if i:
                pe.wait_ge(pv_taken, i)
            half = slice(64 * (h % 2), 64 * (h % 2) + 64)
            for k in range(KT):
                mm = pe.matmul(bank[6][half, :], v[:, k, h * HD:(h + 1) * HD], probsT[:, k, :],
                               start=(k == 0), stop=(k == KT - 1))
            mm.then_inc(pv_done, 1)

        pe.wait_ge(mod_taken, 1)
        for df, scores in ((0, na_scores), (1, df_scores)):
            ahead = 1 if df else 2
            for u in range(ahead):
                scores(u)
            for u, (h, t) in enumerate(UNITS):
                n = df * NU + u
                if u + ahead < NU:
                    scores(u + ahead)
                if t == 0 and n:
                    weighted(n // TT - 1)
                pe.wait_ge(probs_ready, n + 1)
                if n > 0:
                    pe.wait_ge(probsT_act, n)
                    pe.wait_ge(probsT_dve, n)
                p = p_df[u % 2][:, 0] if df else p_na[u % 2]
                for k in range(KT):
                    mm = pe.transpose(tpair[:, k * P:(k + 1) * P], p[:, k * P:(k + 1) * P], ident[:])
                mm.then_inc(transposed, 1)
                i = N_MODA + n // TT
                if t == 2:
                    arrived(i + N_IN)
                    if i > N_MODA:
                        pe.wait_ge(pv_taken, i - N_MODA)
                    mod_sums(slot(i + N_IN))
                if t == 3:
                    pe.wait_ge(mod_copied, i + 1)
                    for j in range(4):
                        at = 32 + 4 * (i - N_MODA) + j
                        mm = pe.matmul(bank[7][:, at:at + 1], mod_row[:, j * P:(j + 1) * P], cond_sel[:, 0:1], start=True, stop=True)
                    mm.then_inc(mod_turned, 1)
        weighted(2 * H - 1)
        dfsq = [region(3072 + 512 * i, T) for i in range(2)]
        S.at[squares.name] = 2 * KD
        for i in range(2):
            S.wait(squares)
            pe.matmul(bank[i], tab["same"], dfsq[i], start=True, stop=True).then_inc(summed, 1)

        ftA, ftY = region(0, TT, 2, 256), region(2048, 2, T)
        for t in range(TT):
            if t >= 2:
                pe.wait_ge(ft_chan_taken, t - 1)
            for i in range(2):
                mm = pe.matmul(bank[2 + t % 2][:, i * 256:(i + 1) * 256], uft[:, i, t * P:(t + 1) * P],
                               tab["dft_chan"], start=True, stop=True)
            mm.then_inc(ft_chan_done, 1)
        n2 = n0 + N_IN + N_MODB
        arrived(n2)
        pe.wait_ge(ft_chan_taken, TT)
        dft = slot(n2).rearrange("p (c k) n -> p c k n", c=2)
        for i in range(2):
            for c in range(2):
                for t in range(TT):
                    mm = pe.matmul(bank[4 + i], ftA[:, t, i, c * P:(c + 1) * P], dft[:, c, t, :],
                                   start=(c == 0 and t == 0), stop=(c == 1 and t == TT - 1))
            mm.then_inc(ft_tok_done, 1)
        pe.wait_ge(ft_tok_taken, 2)
        pe.wait_ge(s_ftw, 16)
        pe.wait_ge(rstd_ready, 4)
        for n in range(2):
            for i in range(2):
                mm = pe.matmul(bank[n], ftw[:, i, n * P:(n + 1) * P], ftY[:, i], start=(i == 0), stop=(i == 1))
            mm.then_inc(ft_done, 1)

        pe.wait_ge(ft_taken, 2)
        for j, (sq, (x, n)) in enumerate(zip(l2sq, l2jobs)):
            S.wait(squares)
            pe.matmul(bank[j][:, 0:n], tab["same"], sq[:, 0:n], start=True, stop=True).then_inc(summed, 1)
        S.wait(g_ready)
        gf = g_.rearrange("p t x -> p (t x)")
        for j, m in enumerate((tab["tri"][:, 0:P], tab["tri"][:, P:2 * P], tab["same"])):
            pe.matmul(bank[6][:, 48 * j:48 * j + 48], m, gf, start=True, stop=True)
        pe.wait_ge(rstd_ready, 10)
        for c in range(2):
            half = slice(64 * c, 64 * c + 64)
            mm = pe.matmul(bank[4 + c][:, 0:48], ones[half, :], gf[half, :], start=True, stop=True)
        mm.then_inc(gc_done, 1)
        pe.wait_ge(normed, 6)
        pe.wait_ge(gc_exp, 6)
        pe.wait_ge(dn_coef, 1)
        halves = [slice(0, 64), slice(64, 128)]
        PR = [(d, h) for d in range(2) for h in range(H)]

        def products(dst, left, right):
            for h in range(H):
                for d in range(2):
                    for r, e in zip(halves, (d, 1 - d)):
                        mm = pe.matmul(dst[r, e, h], left[r, e, h], right(r, e, h), start=True, stop=True)
            return mm

        for n, pair in enumerate(PAIRS):
            for q, t in enumerate(pair):
                if n:
                    pe.wait_ge(uw_taken, 6 * n)
                tk = slice(t * P, t * P + P)
                for j, x in enumerate((dk[:, 0, tk], dk[:, 1, tk], dv[:, 0, tk], dv[:, 1, tk])):
                    mm = pe.transpose(dnT[q][:, j * P:(j + 1) * P], x, ident[:])
                mm.then_inc(tok_done, 1)
            for q, t in enumerate(pair):
                S.wait(gtri_ready)
                pe.matmul(dnG[q], tab["same"], dn[q]["gtri"].rearrange("p d h c -> p (d h c)"), start=True, stop=True)\
                  .then_inc(grow_done, 1)
                kk = dnK[:, q]
                for h in range(H):
                    f = halves[h % 2]
                    for c, r in enumerate(halves):
                        tk = slice(t * P + CH * c, t * P + CH * c + CH)
                        mm = pe.matmul(kk[r, 0, h // 2, h % 2], dk[f, h // 2, tk], dk[f, h // 2, tk], start=True, stop=True)
                        if t < TT:
                            mm = pe.matmul(kk[r, 1, h // 2, h % 2], dk[f, h // 2, tk], dq[f, h // 2, tk], start=True, stop=True)
                mm.then_inc(kk_done, 1)
            for q, t in enumerate(pair):
                if t < TT:
                    pe.wait_ge(decay_arg, 2 * n + q + 1)
                    S.wait(gb_ready)
                    for d in range(2):
                        for h in range(H):
                            mm = pe.matmul(dnG[q][halves[h % 2], (2 * d + h // 2) * P:(2 * d + h // 2 + 1) * P],
                                           dn[q]["gb"][:, d, h], tab["tri"][:, d * P:(d + 1) * P], start=True, stop=True)
                    mm.then_inc(gq_done, 1)
            for s in range(6):
                for q, t in enumerate(pair):
                    B = dn[q]
                    S.wait(ns_ready)
                    if s == 0:
                        pe.wait_ge(tok_taken, 2 * n + q + 1)
                        if t < TT:
                            S.wait(gq_exp)
                        right = lambda r, d, h: tab["eye64"][r, :]
                    else:
                        S.wait(x_ready)
                        right = lambda r, d, h: B["X"][r, d, h]
                    products(v4(dnA[q]), B["ns"], right).then_inc(y_done, 1)
                for q, t in enumerate(pair):
                    B = dn[q]
                    if s == 0:
                        pe.wait_ge(x_ready, 10 * n + q + 1)
                        products(v4(dnB[q]), B["X"], lambda r, d, h: tab["eye64"][r, :]).then_inc(w_done, 1)
                        continue
                    S.wait(y_ready)
                    S.wait(w_seed if s == 1 else w_ready)
                    if s < 5:
                        products(v4(dnA[q]), B["W"], lambda r, d, h: B["Y"][r, d, h]).then_inc(x_done, 1)
                    products(v4(dnB[q]), B["Y"], lambda r, d, h: B["W"][r, d, h]).then_inc(w_done, 1)
            for q, t in enumerate(pair):
                B = dn[q]
                S.wait(w_ready)
                products(v4(dnA[q]), B["W"], lambda r, d, h: B["vb"][r, d, h]).then_inc(uw_done, 1)
                wt = [dnB[q][:, c, 0:2 * P].rearrange("p (d a x) -> p d a x", d=2, a=2) for c in range(2)]
                for d, h in PR:
                    for c, r in enumerate(halves):
                        mm = pe.matmul(wt[c][halves[h % 2], d, h // 2], B["kb"][r, d, h], B["W"][r, d, h],
                                       start=True, stop=True)
                mm.then_inc(uw_done, 1)

        pe.wait_ge(uw_taken, 6 * len(PAIRS))
        pe.wait_ge(qk_ready, TT)
        for i in range(STEPS):
            at = [chunk_at(d, i) for d in range(2)]
            s_ = state[i % 2]
            for d, (t, c) in enumerate(at):
                S.wait(state_ready, (1 if d == 0 else 0) if i == 0 else 1)
                for h in range(H):
                    f = halves[h % 2]
                    mm = pe.matmul(bank[2 * d + h % 2][halves[c], (h // 2) * CH:(h // 2 + 1) * CH],
                                   wT[f, t, c, d, h // 2], s_[f, d, h // 2], start=True, stop=True)
                mm.then_inc(v_done, 1)
            if i >= 4:
                for d, (t, c) in enumerate(at):
                    if i > 4:
                        S.wait(o_taken)
                    for h in range(H):
                        f = halves[h % 2]
                        mm = pe.matmul(bank[6 + d][f, (h // 2) * CH:(h // 2 + 1) * CH], s_[f, d, h // 2],
                                       qdec[f, t, d, h // 2, c * CH:(c + 1) * CH],
                                       start=(h < 2), stop=False, skip_group_check=True)
                    mm.then_inc(oq_done, 1)
            for d, (t, c) in enumerate(at):
                S.wait(vnew_ready)
                for h in range(H):
                    mm = pe.matmul(bank[4 + d][halves[h % 2], (h // 2) * CH:(h // 2 + 1) * CH], kdec[halves[c], t, d, h],
                                   vnew[halves[c], d, h], start=True, stop=True)
                mm.then_inc(sd_done, 1)
            if i >= 4:
                for d, (t, c) in enumerate(at):
                    S.wait(oq_done)
                    for h in range(H):
                        mm = pe.matmul(bank[6 + d][halves[h % 2], (h // 2) * CH:(h // 2 + 1) * CH], vnew[halves[c], d, h],
                                       qkT[halves[c], t, d, h], start=False, stop=True, skip_group_check=True)
                    mm.then_inc(o_done, 1)
        for i in range(2):
            S.wait(squares)
            pe.matmul(bank[i], tab["same"], dn_out[:, 1, i], start=True, stop=True).then_inc(summed, 1)

        pe.wait_ge(dn_ready, 2)
        for n in range(KD):
            if n % 4 == 0:
                arrived(FRONT + n // 4)
            if n >= 4:
                pe.wait_ge(out_taken, n - 3)
            w = slot(FRONT + n // 4)
            for k in range(KD):
                mm = pe.matmul(bank[2 + n % 4], w[:, k, (n % 4) * P:(n % 4 + 1) * P], mix[:, k], start=(k == 0),
                               stop=(k == KD - 1))
            mm.then_inc(out_done, 1)
        for k in range(KD):
            S.wait(squares)
            mm = pe.matmul(bank[6], ones[:], moe_sq[:, k], start=(k == 0), stop=(k == KD - 1))
        mm.then_inc(summed, 1)
        pe.wait_ge(s_wr, 16)
        pe.wait_ge(h2_ready, KD)
        for t in range(TT):
            for k in range(KD):
                mm = pe.matmul(bank[7][:, t * NE:(t + 1) * NE], h2[:, k, t * P:(t + 1) * P], wr[:, k, :],
                               start=(k == 0), stop=(k == KD - 1))
        mm.then_inc(logit_done, 1)
        pe.wait_ge(aff_ready, 1)
        for t in range(TT):
            mm = pe.transpose(bank[6][0:NE, t * P:(t + 1) * P], aff[:, t, :], ident[:])
        mm.then_inc(affT_done, 1)
        for n in range(TT * 2):
            t, half = n // 2, n % 2
            if n >= 4:
                pe.wait_ge(tok2_taken, n - 3)
            for j in range(4):
                mm = pe.transpose(bank[n % 4][:, j * P:(j + 1) * P], h2[:, 4 * half + j, t * P:(t + 1) * P], ident[:])
            mm.then_inc(tok2_done, 1)
        pe.wait_ge(slotT_ready, 1)
        for t in range(TT):
            mm = pe.transpose(bank[7][:, t * NE:(t + 1) * NE], count[0:NE, t * P:(t + 1) * P], ident[0:NE, 0:NE])
        mm.then_inc(slot_done, 1)
        pe.wait_ge(slot_ready, 1)
        pe.wait_ge(tok2_taken, 2 * TT)

        with pe.Fori(0, NE) as e:
            E = Turn(pe, e, PER_E, {added.name: 1})

            def chunk(j):
                n = MOE0 + j
                pe.wait_ge(slot_in[n % SLOTS], e * (16 * EC // SLOTS) + 16 * (n // SLOTS + 1))
                return ring[:, n % SLOTS, :]
            E.wait(pick_ready)
            for t in range(TT):
                for s in range(2):
                    mm = pe.matmul(bank[4][64 * s:64 * s + 64, :], pick[:, t, :], h_tok[:, t, 512 * s:512 * s + 512],
                                   start=(t == 0), stop=(t == TT - 1))
            E.sig(mm, gathered)
            for t in range(TT):
                mm = pe.transpose(bank[6][:, t * P:(t + 1) * P], pickg[:, t].rearrange("p a c -> p (a c)"), ident[:])
            E.sig(mm, pgT_done)
            E.wait(x_tok_ready)
            for i in range(4):
                mm = pe.transpose(bank[0][:, i * P:(i + 1) * P], x_tok[:, i * P:(i + 1) * P], ident[:])
            E.sig(mm, xgT_done)
            E.wait(xg_ready)
            for j in range(2):
                if j == 1:
                    pe.wait_ge(added, e * PER_E["added"] + 1)
                for b in (j, 2 + j):
                    for kk in range(2):
                        w = chunk(4 * j + 2 * (b // 2) + kk).rearrange("p (k s c) -> p k s c", k=4, s=2)
                        for k in range(4):
                            for s in range(2):
                                mm = pe.matmul(bank[b][64 * s:64 * s + 64, :], xg[:, 4 * kk + k, :], w[:, k, s, :],
                                               start=(kk == 0 and k == 0), stop=(kk == 1 and k == 3))
                        E.sig(mm, w_used)
            E.wait(pgT_ready)
            for j in range(2):
                E.wait(hid_ready)
                if j == 1:
                    E.wait(hidT_ready)
                for i in range(4):
                    mm = pe.transpose(bank[6][:, i * P:(i + 1) * P], hid[:, j, i * P:(i + 1) * P], ident[:])
                E.sig(mm, hidT_done)
            for c in range(4):
                w = chunk(8 + c).rearrange("p (f d) -> p f d", f=4)
                if c == 2:
                    E.wait(hidT_ready)
                for f in range(4):
                    left_ = hidT[:, 4 * (c // 2) + f, 64 * (c % 2):64 * (c % 2) + 64]
                    for s in range(2):
                        mm = pe.matmul(bank[4][64 * s:64 * s + 64, :], left_, w[:, f, 512 * s:512 * s + 512],
                                       start=(c == 0 and f == 0), stop=(c == 3 and f == 3))
                E.sig(mm, w_used)
            E.wait(y_ready_e)
            for n in range(KD):
                s = n % 2
                if n >= 4:
                    E.wait(added)
                half = slice(64 * s, 64 * s + 64)
                mm = pe.matmul(bank[SCATTER[n % 4]], ysb[half, (n // 2) * P:(n // 2 + 1) * P], pgT[half, :], start=True, stop=True)
                E.sig(mm, scattered)
            E.end()
        for k in range(KD):
            S.wait(squares)
            mm = pe.matmul(bank[0], ones[:], h2[:, k], start=(k == 0), stop=(k == KD - 1))
        mm.then_inc(summed, 1)


        pe.wait_ge(rstd_ready, 14)
        with pe.Fori(0, LAYERS) as l:
            E = Turn(pe, l, per_l, before_l)

            def chunk_in(j):
                n = L0 + j
                pe.wait_ge(slot_in[n % SLOTS], l * (16 * NLC // SLOTS) + 16 * (n // SLOTS + 1))

            def norm_sum(dst, srcs):
                m = srcs[0].shape[0]
                for i, x in enumerate(srcs):
                    E.wait(Ls["l_sq"])
                    mm = pe.matmul(dst, ones[0:m, 0:m], x, start=(i == 0), stop=(i == len(srcs) - 1))
                E.sig(mm, Ls["l_sum"])

            def lin(g):
                ch, kind, col, dst = LIN[g]
                b = lin_bank(g)
                if g >= 4:
                    E.upto(Ls["lin_taken"], g - 3)
                if kind == "q":
                    for i in range(2):
                        mm = pe.matmul(b, wq[:, i, col * QK_HEAD:(col + 1) * QK_HEAD], qlat[:, i], start=(i == 0), stop=(i == 1))
                elif kind == "k":
                    mm = pe.matmul(b, wkv[:, col, 0:QK_NOPE], kvlat, start=True, stop=True)
                elif kind == "v":
                    mm = pe.matmul(b.rearrange("p (h c) -> p h c", h=H), kvlat[:, col * P:(col + 1) * P],
                                   wkv[:, :, QK_NOPE:], start=True, stop=True)
                else:
                    w = layer_slot(ch)
                    for k in range(KD):
                        se = dict(start=(k == 0), stop=(k == KD - 1))
                        if g == 0:
                            E.upto(Ls["l_h"], k + 1)
                        if kind == "V":
                            mm = pe.matmul(b, hT[:, k, col * P:(col + 1) * P], w[:, k, 256:512], **se)
                        else:
                            mm = pe.matmul(b, w[:, k, col:col + (QK_ROPE if kind == "pe" else P)], hT[:, k], **se)
                E.sig(mm, Ls["lin_done"])

            norm_sum(bank[0], [l_sqb[:, k] for k in range(KD)])
            for g in range(12):
                if g in (0, 4, 10):
                    chunk_in(LIN[g][0])
                lin(g)
            norm_sum(bank[0], [Q[0], Q[1]])
            norm_sum(bank[5], [Q[2]])
            E.upto(Ls["v_scaled"], TT)
            E.upto(Ls["wsp_ready"], 1)
            E.upto(Ls["l_rstd"], 3)
            for i in range(2):
                for t in range(TT):
                    for o in range(2):
                        h = 2 * i + o
                        mm = pe.matmul(bank[5 + i][64 * o:64 * o + 64, t * P:(t + 1) * P], vtok[:, t, h * HD:(h + 1) * HD],
                                       wsp[:, h], start=True, stop=True)
                E.sig(mm, Ls["sgu_done"])
            E.upto(Ls["qn_ready"], 3)
            for g in range(12, 24):
                if g == 23:
                    E.upto(Ls["pool_ready"], 1)
                lin(g)
            for i in range(2):
                for o in range(2):
                    half = slice(64 * o, 64 * o + 64)
                    mm = pe.matmul(bank[(7, 0)[i]][half], wpool[half, i], pm[half, i], start=True, stop=True)
                E.sig(mm, Ls["pool_done"])
            E.upto(Ls["pool_taken"], 2)
            for j in range(9):
                if j < 8:
                    if j >= 2:
                        E.upto(Ls["l_rstd"], 3 + j - 1)
                    norm_sum(head_bank[j % 2][0:QK_HEAD], [Q[j % 2][0:QK_HEAD]])
                if j >= 1:
                    i = j - 1
                    E.upto(Ls["turn_in"], i + 1)
                    if i >= 2:
                        E.upto(Ls["roped"], i - 1)
                    E.sig(pe.matmul(turn_bank[i % 2][0:QK_HEAD], tab2["turn"][0:QK_HEAD, 0:QK_HEAD], HEADS[i],
                                    start=True, stop=True), Ls["turned"])
            E.upto(Ls["lin_taken"], 24)
            E.upto(Ls["roped"], 8)

            def scores(u):
                h, t = UNITS[u]
                if u >= 2:
                    E.upto(Ls["sc_taken"], u - 1)
                n = (t + 1) * P
                E.sig(pe.matmul(bank[1 + u % 2][:, 0:n], qh[0:QK_HEAD, h, t * P:n], kh[0:QK_HEAD, h, 0:n],
                                start=True, stop=True), Ls["sc_done"])
            def weighted(h):
                E.upto(Ls["pt_taken"], TT * (h + 1))
                if h:
                    E.upto(Ls["pvl_taken"], h)
                for k in range(TT):
                    mm = pe.matmul(bank[4][:, k * P:], vh[:, k, h * VH:(h + 1) * VH], pT2[:, k, k * P:],
                                   start=(k == 0), stop=(k == TT - 1))
                E.sig(mm, Ls["pvl_done"])

            scores(0)
            scores(1)
            for u, (h, t) in enumerate(UNITS):
                if u + 2 < NU:
                    scores(u + 2)
                if t == 0 and h:
                    weighted(h - 1)
                E.upto(Ls["pr_ready"], u + 1)
                if u:
                    E.upto(Ls["pt_taken"], u)
                for k in range(t + 1):
                    mm = pe.transpose(bank[3][:, k * P:(k + 1) * P], p2[u % 2][:, k * P:(k + 1) * P], ident[:])
                E.sig(mm, Ls["tr_done"])
            weighted(H - 1)
            for b, lo, hi in ((0, 0, 4), (5, 4, 6), (6, 6, 8)):
                norm_sum(bank[b], [osq[:, k] for k in range(lo, hi)])
            for n in range(KD):
                j = 3 + n // 4
                if n % 4 == 0:
                    chunk_in(j)
                if n >= 4:
                    E.upto(Ls["lo_taken"], n - 3)
                for k in range(KD):
                    if n == 0:
                        E.upto(Ls["mixn"], k + 1)
                    mm = pe.matmul(bank[1 + n % 4], layer_slot(j)[:, k, (n % 4) * P:(n % 4 + 1) * P], mix[:, k],
                                   start=(k == 0), stop=(k == KD - 1))
                E.sig(mm, Ls["lo_done"])
            norm_sum(bank[0], [l_sqb[:, k] for k in range(KD)])
            for f in range(FT):
                j = 5 + f // 2
                if f % 2 == 0:
                    chunk_in(j)
                w = layer_slot(j).rearrange("p (m k n) -> p m k n", m=2, k=KD)
                if f >= 2:
                    E.upto(Ls["hidden"], f - 1)
                for m, s in ((0, "gate_done"), (1, "up_done")):
                    for k in range(KD):
                        if f == 0 and m == 0:
                            E.upto(Ls["l_h"], KD + k + 1)
                        mm = pe.matmul(bank[2 * m + f % 2], w[:, m, k, (f % 2) * P:(f % 2 + 1) * P], hT[:, k],
                                       start=(k == 0), stop=(k == KD - 1))
                    E.sig(mm, Ls[s])
            for n in range(KD):
                chunk_in(16 + n)
                w = layer_slot(16 + n).rearrange("p (f n) -> p f n", f=FT)
                if n >= 2:
                    E.upto(Ls["down_taken"], n - 1)
                for f in range(FT):
                    if n == 0:
                        E.upto(Ls["hidden"], f + 1)
                    mm = pe.matmul(bank[4 + n % 2], w[:, f, :], hidden[:, f], start=(f == 0), stop=(f == FT - 1))
                E.sig(mm, Ls["down_done"])
            E.end()

    ctx.close()


def laid_out(i):
    v = {k: np.asarray(x) for k, x in i.items()}

    def col(x):
        return x.reshape(-1, P).T

    d = {}
    cond = np.stack([v["c"][0], v["c_ctx"]], -1).reshape(KD, P, 2).transpose(1, 0, 2).reshape(P, 16)
    conv = v["dn_conv_w"][0].reshape(CONV, 6, P).transpose(2, 1, 0).reshape(P, 30)
    twice = lambda x: np.concatenate([x, x])[:, None]
    d["par"] = np.concatenate([cond, col(v["b_mod"][0]), col(v["norm1_g"][0]), col(v["norm2_g"][0]),
                               col(v["final_norm_g"]), conv, twice(v["dn_norm_g"][0]), twice(v["df_norm_g"][0]),
                               (np.arange(P)[:, None] % 32 == np.arange(2)).astype(np.float32)], 1)
    d["rows"] = np.concatenate([v["dn_a_log"][0].ravel(), v["dn_dt_bias"][0].ravel(), v["df_lambda"][0].ravel()])
    d["xT"], d["ctxT"] = v["x"][0].T, v["ctx"][0].T
    d["w_mod"], d["w_in"] = v["w_mod"][0], v["w_in"][0]
    d["w_out"], d["ft_w"] = v["w_out"][0], v["ft_w"][0]
    pad = np.zeros((H, 15, 2 * GRID - 1), np.float32)
    pad[:, :, GRID - 1 - NDX // 2:GRID + NDX // 2] = v["na_rpb"][0]
    d["rpb"] = np.stack([pad[:, :, GRID - 1 - q:2 * GRID - 1 - q] for q in range(GRID)], 1)
    d["const"], d["dft"], d["ident"] = first_constants()[0], dft_table(), np.eye(P, dtype=np.float32)
    d["w_router"] = v["w_router"][0]
    d["const2"] = later_constants()[0]
    up = np.stack([v["w_gate"][0], v["w_up"][0]], 1).reshape(NE, 2, 2, 4, P, 2, 2, 512)
    up = up.transpose(0, 6, 1, 2, 4, 3, 5, 7).reshape(NE, 8, P, SLOT)
    down = v["w_down"][0].reshape(NE, 2, 2, 4, P, D)
    down = down.transpose(0, 2, 1, 4, 3, 5).reshape(NE, 4, P, SLOT)
    d["w_moe"] = np.concatenate([up, down], 1)
    d["positions"] = v["positions_2"][0]
    small = []
    for l in range(LAYERS):
        tall = lambda x: np.concatenate([x, np.zeros(P - len(x), x.dtype)])[:, None]
        w = {k[:-2]: x[l] for k, x in v.items() if k.endswith("_2") and k != "positions_2"}
        p_ = [col(w[k]) for k in ("g_mix_norm", "g_ffn_norm", "g_out_mla", "g_out_sgu", "g_out_pool", "g_q_lat",
                                  "g_kv_lat", "g_sgu_v", "pool_scale")]
        p_ += [tall(w["g_q_head"]), tall(w["g_k_head"]), np.zeros((P, 7), np.float32)]
        pairs = lambda x: np.concatenate([x[0::2], x[1::2]], 1)
        p_.append(w["w_q_up"].reshape(2, P, -1).transpose(1, 0, 2).reshape(P, -1))
        p_.append(w["w_kv_up"])
        p_.append(pairs(w["w_pool"]).transpose(1, 0, 2).reshape(P, -1))
        p_.append(w["w_spatial"].transpose(2, 0, 1).reshape(P, -1))
        b = np.repeat(w["b_spatial"][:, None], HD, 1)
        p_.append(pairs(b).transpose(1, 0, 2).reshape(P, -1))
        small.append(np.concatenate(p_, 1))
    d["small_2"] = np.stack(small)
    assert d["small_2"].shape[2] == L_ALL
    d["w_in_2"], d["w_out_2"] = v["w_in_2"], v["w_out_2"]
    gu = np.stack([v["w_gate_2"], v["w_up_2"]], 1).reshape(LAYERS, 2, KD, P, 11, 256)
    d["w_gu_2"] = gu.transpose(0, 4, 3, 1, 2, 5).reshape(LAYERS, 11, P, SLOT)
    dn = v["w_down_2"].reshape(LAYERS, FT, P, KD, P)
    d["w_dn_2"] = dn.transpose(0, 3, 2, 1, 4).reshape(LAYERS, KD, P, FF)
    return {k: np.ascontiguousarray(x) for k, x in d.items()}


def kernel(**inputs):
    import concourse.bacc as bacc
    from concourse.bass_utils import run_bass_kernel_spmd

    nc = bacc.Bacc("TRN2", target_bir_lowering=False, num_devices=1)
    arrays = laid_out(inputs)
    aps = {k: nc.dram_tensor(f"in_{k}", x.shape, mybir.dt.from_np(x.dtype), kind="ExternalInput").ap()
           for k, x in arrays.items()}
    out = nc.dram_tensor("outT", (D, T), F32, kind="ExternalOutput").ap()
    build(nc, aps, out)
    r = run_bass_kernel_spmd(nc, [{f"in_{k}": x for k, x in arrays.items()}], core_ids=[0])
    return np.ascontiguousarray(r.results[0]["outT"].T)[None]
```
